# Optimizing a Trainium2 kernel written in Bass

```python
import jax, jax.numpy as jnp
from jax import lax
import numpy as np

D_MODEL = 1024
BATCH = 1
SEQ = 512
DEPTH = 2

N_HEADS = 16
HEAD_DIM = D_MODEL // N_HEADS
D_FF = -(-8 * D_MODEL // (3 * 256)) * 256
BLOCK_Q = 128
N_A = DEPTH // 2
N_B = DEPTH - N_A
EPS = 1e-6

kernel_name = "yoco_stickbreak_fox_adaln"

def rms_norm(x, g):
    xf = x.astype(jnp.float32)
    y = xf * lax.rsqrt(jnp.mean(xf * xf, axis=-1, keepdims=True) + EPS)
    return (y * g.astype(jnp.float32)).astype(x.dtype)

def modulate(h, shift, scale):
    return h * (1.0 + scale[:, None, :]) + shift[:, None, :]

def split_heads(t):
    b, s, _ = t.shape
    return t.reshape(b, s, N_HEADS, HEAD_DIM).transpose(0, 2, 1, 3)

def merge_heads(t):
    b, h, s, d = t.shape
    return t.transpose(0, 2, 1, 3).reshape(b, s, h * d)

def to_blocks(t):
    b, h, s = t.shape[:3]
    t = t.reshape((b, h, s // BLOCK_Q, BLOCK_Q) + t.shape[3:])
    return jnp.moveaxis(t, 2, 0)

def from_blocks(t):
    nb, b, h, bq, d = t.shape
    return jnp.moveaxis(t, 0, 2).reshape(b, h, nb * bq, d)

def stick_breaking_attention(q, k, v):
    s_len = q.shape[2]
    scale = HEAD_DIM ** -0.5
    kpos = jnp.arange(s_len)

    def block(args):
        qb, start = args
        z = jnp.einsum('bhqd,bhkd->bhqk', qb, k).astype(jnp.float32) * scale
        qpos = start + jnp.arange(BLOCK_Q)
        mask = kpos[None, :] < qpos[:, None]
        log_1m = jnp.where(mask, jax.nn.log_sigmoid(-z), 0.0)
        log_rest = lax.cumsum(log_1m, axis=3, reverse=True) - log_1m
        a = jnp.where(mask, jnp.exp(jax.nn.log_sigmoid(z) + log_rest), 0.0)
        return jnp.einsum('bhqk,bhkd->bhqd', a.astype(v.dtype), v)

    starts = jnp.arange(s_len // BLOCK_Q) * BLOCK_Q
    return from_blocks(lax.map(block, (to_blocks(q), starts)))

def forgetting_attention(q, k, v, fcum):
    s_len = q.shape[2]
    scale = HEAD_DIM ** -0.5
    kpos = jnp.arange(s_len)

    def block(args):
        qb, fq, start = args
        logit = jnp.einsum('bhqd,bhkd->bhqk', qb, k).astype(jnp.float32) * scale
        logit = logit + fq[..., :, None] - fcum[:, :, None, :]
        qpos = start + jnp.arange(BLOCK_Q)
        mask = kpos[None, :] <= qpos[:, None]
        p = jax.nn.softmax(jnp.where(mask, logit, -jnp.inf), axis=-1)
        return jnp.einsum('bhqk,bhkd->bhqd', p.astype(v.dtype), v)

    starts = jnp.arange(s_len // BLOCK_Q) * BLOCK_Q
    return from_blocks(lax.map(block, (to_blocks(q), to_blocks(fcum), starts)))

def swiglu(h, w_in, w_down):
    g, u = jnp.split(h @ w_in, 2, axis=-1)
    return (jax.nn.silu(g) * u) @ w_down

def setup_inputs(seed: int = 0) -> dict:
    key = jax.random.key(seed)
    ks = jax.random.split(key, 20)
    D, H, F, dh = D_MODEL, N_HEADS, D_FF, HEAD_DIM
    f32 = jnp.float32

    def w(k, shape, fan_in, mult=1.0):
        return jax.random.normal(k, shape, f32) * (mult * fan_in ** -0.5)

    def gain(k, shape):
        return 1.0 + 0.02 * jax.random.normal(k, shape, f32)

    return {
        "x": jax.random.normal(ks[0], (BATCH, SEQ, D), f32),
        "c": jax.random.normal(ks[1], (BATCH, D), f32),
        "ada_w": w(ks[2], (DEPTH, D, 6 * D), D, 0.5),
        "ada_b": 0.02 * jax.random.normal(ks[3], (DEPTH, 6 * D), f32),
        "norm_attn_g": gain(ks[4], (DEPTH, D)),
        "norm_ffn_g": gain(ks[5], (DEPTH, D)),
        "w_ffn_in": w(ks[6], (DEPTH, D, 2 * F), D),
        "w_ffn_down": w(ks[7], (DEPTH, F, D), F),
        "sb_w_qkv": w(ks[8], (N_A, D, 3 * D), D),
        "sb_w_o": w(ks[9], (N_A, D, D), D),
        "kv_ada_w": w(ks[10], (D, 2 * D), D, 0.5),
        "kv_ada_b": 0.02 * jax.random.normal(ks[11], (2 * D,), f32),
        "kv_norm_g": gain(ks[12], (D,)),
        "w_kvf": w(ks[13], (D, 2 * D + H), D),
        "b_f": jax.random.uniform(ks[14], (H,), f32, 1.0, 4.0),
        "k_norm_g": gain(ks[15], (dh,)),
        "fox_w_q": w(ks[16], (N_B, D, D), D),
        "q_norm_g": gain(ks[17], (N_B, dh)),
        "fox_w_o": w(ks[18], (N_B, D, D), D),
    }

def reference(x, c, ada_w, ada_b, norm_attn_g, norm_ffn_g, w_ffn_in, w_ffn_down,
              sb_w_qkv, sb_w_o, kv_ada_w, kv_ada_b, kv_norm_g, w_kvf, b_f,
              k_norm_g, fox_w_q, q_norm_g, fox_w_o):
    D = D_MODEL
    c_act = jax.nn.silu(c.astype(jnp.float32)).astype(x.dtype)
    k_sh = v_sh = fcum = None
    for layer in range(DEPTH):
        mod = c_act @ ada_w[layer] + ada_b[layer]
        sh_a, sc_a, g_a, sh_f, sc_f, g_f = jnp.split(mod, 6, axis=-1)
        if layer < N_A:
            h = modulate(rms_norm(x, norm_attn_g[layer]), sh_a, sc_a)
            q, k, v = jnp.split(h @ sb_w_qkv[layer], 3, axis=-1)
            o = stick_breaking_attention(split_heads(q), split_heads(k), split_heads(v))
            mix = merge_heads(o) @ sb_w_o[layer]
        else:
            if layer == N_A:
                kv_shift, kv_scale = jnp.split(c_act @ kv_ada_w + kv_ada_b, 2, axis=-1)
                hk = modulate(rms_norm(x, kv_norm_g), kv_shift, kv_scale)
                proj = hk @ w_kvf
                k_sh = rms_norm(split_heads(proj[..., :D]), k_norm_g)
                v_sh = split_heads(proj[..., D:2 * D])
                log_f = jax.nn.log_sigmoid(proj[..., 2 * D:].astype(jnp.float32) + b_f)
                fcum = lax.cumsum(log_f, axis=1).transpose(0, 2, 1)
            i = layer - N_A
            h = modulate(rms_norm(x, norm_attn_g[layer]), sh_a, sc_a)
            q = rms_norm(split_heads(h @ fox_w_q[i]), q_norm_g[i])
            o = forgetting_attention(q, k_sh, v_sh, fcum)
            mix = merge_heads(o) @ fox_w_o[i]
        x = x + g_a[:, None, :] * mix
        h = modulate(rms_norm(x, norm_ffn_g[layer]), sh_f, sc_f)
        x = x + g_f[:, None, :] * swiglu(h, w_ffn_in[layer], w_ffn_down[layer])
    return x


_drawn_inputs = setup_inputs


def setup_inputs(seed=0):
    import zlib

    import numpy as np

    out = dict(_drawn_inputs(seed))
    spreads = {}
    factors = {'norm_attn_g': 8.0,
     'norm_ffn_g': 6.88,
     'kv_ada_b': 8.0,
     'kv_norm_g': 8.0,
     'k_norm_g': 8.0,
     'q_norm_g': 8.0}
    for name, (base, spread) in spreads.items():
        noise = np.random.default_rng([zlib.crc32(name.encode()), seed]).standard_normal(out[name].shape)
        drawn = base * np.exp(spread * noise) if base else spread * noise
        out[name] = __import__('jax').numpy.asarray(drawn.astype(out[name].dtype))
    for name, factor in factors.items():
        out[name] = (out[name] * factor).astype(out[name].dtype)
    return out
```

```python
from contextlib import ExitStack

import concourse.bass as bass
from concourse import mybir

F32 = mybir.dt.float32
F32R = mybir.dt.float32r
ACT = mybir.ActivationFunctionType
ALU = mybir.AluOpType
AX = mybir.AxisListType

P = 128
SLOTS = 3
EPS = 1e-6
NEG = -(2.0 ** 100)
EXP_LN_SET = 6
N_CONSTS = 20


def after(eng, sem, n):
    if not isinstance(n, int) or n > 0:
        eng.wait_ge(sem, n)


def build(nc, x, c, ada_w, ada_b, norm_attn_g, norm_ffn_g, w_ffn_in, w_ffn_down, sb_w_qkv, sb_w_o,
          kv_ada_w, kv_ada_b, kv_norm_g, w_kvf, b_f, k_norm_g, fox_w_q, q_norm_g, fox_w_o, out):
    _, S, D = x.shape
    FF = w_ffn_down.shape[1]
    H = b_f.shape[0]
    DH = D // H
    KT = D // P
    FT = FF // P
    TB = S // P
    NP = H // 2
    SPAN = [S - P * i for i in range(TB)]
    OFF = [sum(SPAN[:i]) for i in range(TB)]
    PK = sum(SPAN)
    HB = 4
    U_O, U_F, U_D, U_L = 3 * NP, 3 * NP + KT, 3 * NP + KT + 2 * FT, 3 * NP + KT + 2 * FT + 3 * KT
    CH = 512
    M_SHA, M_SCA, M_GA, M_SHF, M_SCF, M_GF = [KT * i for i in range(6)]
    M_KVSH, M_KVSC, M_L1 = 6 * KT, 7 * KT, 8 * KT
    NM = 14 * KT
    G_ATT, G_FFN, G_KV, G_C, G_K, G_Q, G_BF = 0, 2 * KT, 4 * KT, 5 * KT, 6 * KT, 6 * KT + 1, 6 * KT + 2
    NG = 6 * KT + 3
    ADA_F = 4 + NP + 2
    ADA_D = ADA_F + FT // 3
    ADA_N = NM // (CH // P)
    assert ADA_D + KT - 1 == ADA_N
    HBASE = [0, KT, 2 * KT, 4 * KT]

    with ExitStack() as ctx:
        def sem(name):
            return ctx.enter_context(nc.semaphore(name))

        def sb(scope, name, shape, dt=F32):
            return scope.enter_context(nc.sbuf_tensor(name, shape, dt))

        bank = [ctx.enter_context(nc.psum_tensor(f"bank{i}", [P, 512], F32)) for i in range(8)]
        PA, PB = bank[0], bank[1]
        OB = bank[2:4]
        Z = bank[4:8]

        xT = sb(ctx, "xT", [P, KT, S])
        h_hi = sb(ctx, "h_hi", [P, KT, S], F32R)
        h_lo = sb(ctx, "h_lo", [P, KT, S], F32R)
        raw = sb(ctx, "raw", [P, SLOTS, 8, P])
        w_hi = sb(ctx, "w_hi", [P, SLOTS, 8, P], F32R)
        w_lo = sb(ctx, "w_lo", [P, SLOTS, 8, P], F32R)
        sq = sb(ctx, "sq", [P, 2, S])
        tmp = sb(ctx, "tmp", [P, 2, S])
        rstd = sb(ctx, "rstd", [P, S])
        ident = sb(ctx, "ident", [P, P])
        ones = sb(ctx, "ones", [P, P])
        headones = sb(ctx, "headones", [P, P])
        build_tmp = sb(ctx, "build_tmp", [P, P])
        ident_r = sb(ctx, "ident_r", [P, P], F32R)
        ones_r = sb(ctx, "ones_r", [P, P], F32R)
        negones_r = sb(ctx, "negones_r", [P, P], F32R)
        negtri_r = sb(ctx, "negtri_r", [P, P], F32R)
        maskS_r = sb(ctx, "maskS_r", [P, P], F32R)
        maskF_r = sb(ctx, "maskF_r", [P, P], F32R)
        mods = sb(ctx, "mods", [P, NM])
        mod_bias = sb(ctx, "mod_bias", [P, NM])
        gains = sb(ctx, "gains", [P, NG])
        amod = sb(ctx, "amod", [P, 5, KT])
        cact = sb(ctx, "cact", [P, 2, KT])
        epsc = sb(ctx, "epsc", [P, 1])
        stat = sb(ctx, "stat", [P, 4, 4])
        fcum_dram = nc.dram_tensor("fcum_scratch", [2, H, S], F32, kind="Internal").ap()

        l0 = ExitStack()
        ada = sb(l0, "ada", [P, 4, 2, CH])
        acc = sb(l0, "acc", [P, CH])
        start_scope = ExitStack()
        x_nat = sb(start_scope, "x_nat", [P, TB, D])
        rows1 = sb(start_scope, "rows1", [P, P])
        rows2 = sb(start_scope, "rows2", [P, P])
        start_scope.close()
        a0 = ExitStack()
        att = [dict(), dict()]

        def attention_buffers(scope, l):
            b = att[l]
            b["o_hi"] = sb(scope, f"o_hi{l}", [P, NP, S], F32R)
            b["o_lo"] = sb(scope, f"o_lo{l}", [P, NP, S], F32R)
            for n in "qkv":
                b[n + "_hi"] = sb(scope, f"{n}_hi{l}", [P, 2, S], F32R)
                b[n + "_lo"] = sb(scope, f"{n}_lo{l}", [P, 2, S], F32R)
            b["p_hi"] = sb(scope, f"p_hi{l}", [P, PK if l else 2 * S], F32R)
            b["p_lo"] = sb(scope, f"p_lo{l}", [P, PK if l else 2 * S], F32R)
            b["p_at"] = [slice(o, o + SPAN[i]) for i, o in enumerate(OFF if l else [0, S, 0, S])]

        attention_buffers(a0, 0)
        soft = sb(a0, "soft", [P, 2, PK])
        soft_hi = sb(a0, "soft_hi", [P, PK], F32R)
        soft_lo = sb(a0, "soft_lo", [P, PK], F32R)
        wgt = sb(a0, "wgt", [P, 2, S])
        a0.close()
        f0 = ExitStack()
        mid = [dict(), dict()]
        mid[0] = (sb(f0, "mid_hi0", [P, FT, S], F32R), sb(f0, "mid_lo0", [P, FT, S], F32R))
        f0.close()
        l0.close()
        a1 = ExitStack()
        hk_hi = sb(a1, "hk_hi", [P, KT, S], F32R)
        hk_lo = sb(a1, "hk_lo", [P, KT, S], F32R)
        frow = sb(a1, "frow", [P, 2, S], F32R)
        wf_scope = ExitStack()
        wf_hi = sb(wf_scope, "wf_hi", [P, KT, P], F32R)
        wf_lo = sb(wf_scope, "wf_lo", [P, KT, P], F32R)
        wf_raw = sb(wf_scope, "wf_raw", [P, KT, H])
        wf_scope.close()
        attention_buffers(a1, 1)
        prob = sb(a1, "prob", [P, PK])
        a1.close()
        f1 = ExitStack()
        mid[1] = (sb(f1, "mid_hi1", [P, FT, S], F32R), sb(f1, "mid_lo1", [P, FT, S], F32R))
        f1.close()
        e1 = ExitStack()
        out_nat = sb(e1, "out_nat", [P, 2, D])
        e1.close()

        raw_in = [sem(f"raw_in{i}") for i in range(SLOTS)]
        ada_in = [sem(f"ada_in{i}") for i in range(4)]
        x_in, rows_in, wf_in, fcum_out = (sem(n) for n in ("x_in", "rows_in", "wf_in", "fcum_out"))
        out_done = [sem("out_done0"), sem("out_done1")]
        frow_in = [sem("frow_in0"), sem("frow_in1")]
        split_hi, split_lo, unit_used = sem("split_hi"), sem("split_lo"), sem("unit_used")
        consts, rows_zero, wf_zero = sem("consts"), sem("rows_zero"), sem("wf_zero")
        rows_T, cols_w, silu_c = sem("rows_T"), sem("cols_w"), sem("silu_c")
        x_T, x_ready = sem("x_T"), sem("x_ready")
        acc_step, mod_sum, mod_w, amod_w = sem("acc_step"), sem("mod_sum"), sem("mod_w"), sem("amod_w")
        sq_w, sq_sum, rs_ln, rs_w = sem("sq_w"), sem("sq_sum"), sem("rs_ln"), sem("rs_w")
        ht_w, hhi_w, hlo_w = sem("ht_w"), sem("hhi_w"), sem("hlo_w")
        wfs_hi, wfs_lo = sem("wfs_hi"), sem("wfs_lo")
        f_sum, f_y, f_act, f_dve, f_split = sem("f_sum"), sem("f_y"), sem("f_act"), sem("f_dve"), sem("f_split")
        qhi_w, khi_w, vhi_w = sem("qhi_w"), sem("khi_w"), sem("vhi_w")
        qlo_w, klo_w, vlo_w = sem("qlo_w"), sem("klo_w"), sem("vlo_w")
        vT_w, v_T = sem("vT_w"), sem("v_T")
        qk_sq, qk_sum, qk_ln, qk_rs, qk_n = sem("qk_sq"), sem("qk_sum"), sem("qk_ln"), sem("qk_rs"), sem("qk_n")
        z_sum, z_abs, z_exp, z_ln = sem("z_sum"), sem("z_abs"), sem("z_exp"), sem("z_ln")
        soft_w, softhi_w, softlo_w = sem("soft_w"), sem("softhi_w"), sem("softlo_w")
        r_sum, wgt_w, whi_w, phi_w, plo_w, pv = (sem(n) for n in ("r_sum", "wgt_w", "whi_w", "phi_w", "plo_w", "pv"))
        max_w, negmax_w, p_exp, inv_w, p_norm = (sem(n) for n in ("max_w", "negmax_w", "p_exp", "inv_w", "p_norm"))
        ohi_w, olo_w = sem("ohi_w"), sem("olo_w")
        silu_w, m_w, mhi_w, mlo_w = sem("silu_w"), sem("m_w"), sem("mhi_w"), sem("mlo_w")
        y_T, y_w = sem("y_T"), sem("y_w")
        pool_turn = sem("pool_turn")

        def ka(w):
            return w.rearrange("(k p) n -> p k n", p=P)

        WQKV = [(ka(sb_w_qkv[0]), ka(sb_w_qkv[0]), ka(sb_w_qkv[0])), (ka(fox_w_q[0]), ka(w_kvf), ka(w_kvf))]
        CQKV = [(0, D, 2 * D), (0, 0, D)]
        WO = [ka(sb_w_o[0]), ka(fox_w_o[0])]
        DSL = bass.ds
        block = ctx.enter_context(nc.Block())

        @block.sync
        def _(sp):
            def load(u, src, nk=8):
                b, e = u
                after(sp, split_lo, b - 2 + 3 * e)
                sp.dma_start(raw[:, b % SLOTS, 0:nk, :], src).then_inc(raw_in[b % SLOTS], 16)

            sp.wait_ge(rows_zero, 1)
            rows = [(rows1, 0, ada_b[0]), (rows1, 6 * KT, kv_ada_b), (rows1, 8 * KT, ada_b[1]),
                    (rows2, G_ATT, norm_attn_g[0]), (rows2, G_ATT + KT, norm_attn_g[1]),
                    (rows2, G_FFN, norm_ffn_g[0]), (rows2, G_FFN + KT, norm_ffn_g[1]),
                    (rows2, G_KV, kv_norm_g), (rows2, G_C, c[0])]
            for t, r, v in rows:
                n = v.shape[0] // P
                sp.dma_start(t[r:r + n, :], v.rearrange("(r q) -> r q", q=P)).then_inc(rows_in, 16)
            for i, g in ((0, k_norm_g), (1, q_norm_g[0])):
                for j in range(2):
                    sp.dma_start(rows2[G_K + i:G_K + i + 1, j * DH:(j + 1) * DH],
                                 g.rearrange("(r q) -> r q", r=1)).then_inc(rows_in, 16)
            sp.dma_start(rows2[G_BF:G_BF + 1, 0:H], b_f.rearrange("(r q) -> r q", r=1)).then_inc(rows_in, 16)
            sp.dma_start(x_nat[:, :, :], x[0].rearrange("(b p) d -> p b d", p=P)).then_inc(x_in, 16)

            for l in range(2):
                base = U_L * l

                def load_qkv(p, static):
                    for j in range(3):
                        u = (base + j, p)
                        load(u, WQKV[l][j][:, :, DSL(p * P + CQKV[l][j], P)] if not static else
                             WQKV[l][j][:, :, p * P + CQKV[l][j]:p * P + CQKV[l][j] + P])
                load_qkv(0, True)
                with sp.Fori(1, NP) as p:
                    load_qkv(p, False)
                for j in range(KT):
                    load((base + U_O + j, 0), WO[l][:, :, j * P:(j + 1) * P])
                w_in, w_dn = ka(w_ffn_in[l]), ka(w_ffn_down[l])
                load((base + U_F, 0), w_in[:, :, 0:P])
                load((base + U_F + 1, 0), w_in[:, :, FF:FF + P])
                with sp.Fori(0, FT // 3) as i:
                    for r in range(3):
                        load((base + U_F + 2 + 2 * r, 2 * i), w_in[:, :, DSL((3 * i + 1 + r) * P, P)])
                        load((base + U_F + 3 + 2 * r, 2 * i), w_in[:, :, DSL((3 * i + 1 + r) * P + FF, P)])
                with sp.Fori(0, KT) as t:
                    for r, (k0, k1) in enumerate(((0, 8), (8, 16), (16, FT))):
                        load((base + U_D + r, t), w_dn[:, k0:k1, DSL(t * P, P)], k1 - k0)

            for b in range(TB):
                sp.wait_ge(y_w, 2 * (b + 1))
                sp.dma_start(out[0, b * P:(b + 1) * P, :], out_nat[:, b % 2, :]).then_inc(out_done[b % 2], 16)
            for s in range(2):
                sp.wait_ge(out_done[s], 16 * TB // 2)

        @block.gpsimd
        def _(pool):
            pool.memset(rows2[:, :], 0.0).then_inc(rows_zero, 1)
            pool.memset(ident[:, :], 0.0).then_inc(consts, 1)
            pool.memset(ones[:, :], 1.0).then_inc(consts, 1)
            pool.memset(headones[:, :], 0.0).then_inc(consts, 1)
            pool.memset(epsc[:, :], EPS).then_inc(consts, 1)
            pool.wait_ge(consts, 4)
            pool.affine_select(out=ident[:, :], in_=ident[:, :], compare_op=ALU.not_equal, fill=1.0,
                               base=0, pattern=[[-1, P]], channel_multiplier=1).then_inc(consts, 1)
            pool.wait_ge(consts, 5)
            pool.memset(headones[0:DH, 0:DH], 1.0).then_inc(consts, 1)
            pool.wait_ge(consts, 6)
            pool.memset(headones[DH:P, DH:P], 1.0).then_inc(consts, 1)
            pool.wait_ge(consts, 7)
            pool.tensor_copy(ident_r[:, :], ident[:, :]).then_inc(consts, 1)
            pool.tensor_copy(ones_r[:, :], ones[:, :]).then_inc(consts, 1)
            n = 9
            for dst, val, cmp, step in ((negones_r, -1.0, None, 0), (negtri_r, -1.0, ALU.is_ge, -1),
                                        (maskS_r, NEG, ALU.is_ge, -1), (maskF_r, NEG, ALU.is_gt, 1)):
                pool.memset(build_tmp[:, :], val).then_inc(consts, 1)
                n += 1
                pool.wait_ge(consts, n)
                if cmp is not None:
                    pool.affine_select(out=build_tmp[:, :], in_=build_tmp[:, :], compare_op=cmp, fill=0.0,
                                       base=0, pattern=[[step, P]], channel_multiplier=-step).then_inc(consts, 1)
                    n += 1
                    pool.wait_ge(consts, n)
                pool.tensor_copy(dst[:, :], build_tmp[:, :]).then_inc(consts, 1)
                n += 1
                pool.wait_ge(consts, n)
            assert n == N_CONSTS

            def load_ada(ch, w, col):
                wv = w.rearrange("(r k p) n -> r p k n", k=2, p=P)
                for r in range(4):
                    after(pool, acc_step, 8 * ch - 6 + 2 * r)
                    pool.dma_start(ada[:, r, :, :], wv[r][:, :, col]).then_inc(ada_in[r], 16)

            def hi_soft(p):
                for hb in range(2):
                    after(pool, r_sum, 8 * p + 4 * hb)
                    for i in range(HB):
                        o = slice(OFF[i], OFF[i] + SPAN[i])
                        after(pool, soft_w, 8 * p + 4 * hb + i + 1)
                        pool.sem_inc(pool_turn, 1)
                        pool.tensor_copy(soft_hi[:, o], soft[:, hb, o]).then_inc(softhi_w, 1)
                    for i in range(HB):
                        g = 8 * p + 4 * hb + i
                        after(pool, wgt_w, g + 1)
                        after(pool, pv, g - 1)
                        pool.sem_inc(pool_turn, 1)
                        pool.tensor_copy(att[0]["p_hi"][:, att[0]["p_at"][i]],
                                         wgt[:, i % 2, 0:SPAN[i]]).then_inc(whi_w, 1)

            for ch in range(4):
                load_ada(ch, ada_w[0], slice(CH * ch, CH * ch + CH))
            load_ada(4, ada_w[0], slice(CH * 4, CH * 5))
            hi_soft(0)
            with pool.Fori(1, NP) as p:
                load_ada(p + 4, ada_w[0], DSL((p + 4) * CH, CH))
                hi_soft(p)
            with pool.Fori(0, 4) as ch:
                load_ada(ch + 12, kv_ada_w, DSL(ch * CH, CH))
            with pool.Fori(0, 12) as ch:
                load_ada(ch + 16, ada_w[1], DSL(ch * CH, CH))

            pool.wait_ge(unit_used, U_L)
            pool.dma_start(wf_raw[:, :, :], ka(w_kvf)[:, :, 2 * D:2 * D + H]).then_inc(wf_in, 16)
            pool.memset(wf_hi[:, :, :].bitcast(F32), 0.0).then_inc(wf_zero, 1)
            pool.memset(wf_lo[:, :, :].bitcast(F32), 0.0).then_inc(wf_zero, 1)
            pool.wait_ge(f_split, 1)
            pool.dma_start(fcum_dram[0], tmp[0:H, 0, :]).then_inc(fcum_out, 16)
            pool.dma_start(fcum_dram[1], tmp[0:H, 1, :]).then_inc(fcum_out, 16)
            pool.wait_ge(fcum_out, 32)

            def load_frow(s, p, static):
                for hb in range(2):
                    src = fcum_dram[:, 2 * p + hb, :] if static else \
                        fcum_dram[:, DSL(2 * p + hb, 1), :].rearrange("a b s -> a (b s)")
                    pool.dma_start(frow[32 * hb:32 * hb + 2, s, :].bitcast(F32), src).then_inc(frow_in[s], 16)
            load_frow(0, 0, True)
            load_frow(1, 1, True)
            with pool.Fori(1, NP // 2) as i:
                for s in range(2):
                    pool.wait_ge(z_sum, 8 * NP + 8 * (2 * i + s - 1))
                    load_frow(s, 2 * i + s, False)

        @block.tensor
        def _(pe):
            def mm(dst, w, m, start, stop):
                return nc.tensor.matmul(dst, w, m, start=start, stop=stop, skip_group_check=True)

            def passes(dst, wh, wl, xh, xl, start, stop):
                mm(dst, wh, xh, start, False)
                mm(dst, wh, xl, False, False)
                return mm(dst, wl, xh, False, stop)

            def unit(dst, u, xh, xl, nk=8, k0=0, start=True, stop=True, ready=None):
                b, e = u
                s = b % SLOTS
                after(pe, split_lo, b + 1 + 3 * e)
                for k in range(nk):
                    if ready:
                        ready(k0 + k)
                    last = passes(dst, w_hi[:, s, k, :], w_lo[:, s, k, :], xh[:, k0 + k, :], xl[:, k0 + k, :],
                                  start and k == 0, stop and k == nk - 1)
                last.then_inc(unit_used, 1)

            def modulation(ch, b):
                after(pe, acc_step, 8 * ch + 8)
                after(pe, mod_w, ch)
                for j in range(4):
                    last = mm(b[:, j:j + 1], acc[:, j * P:(j + 1) * P], ones[:, 0:1], j == 0, True)
                last.then_inc(mod_sum, 1)

            def square_sum(n, t, s, first=False, last=False):
                after(pe, sq_w, KT * n + t + 1)
                if first and n == 1:
                    pe.wait_ge(mod_w, NP + 4)
                mm(PA[:, :], ones[:, :], sq[:, s, :], first, last).then_inc(sq_sum, 1)

            def scores(l, p, s, h, hb):
                b = att[l]
                r = slice(DH * hb, DH * hb + DH)
                G = 8 * p + 4 * hb
                if hb == 0:
                    after(pe, qlo_w, NP * l + p + 1)
                    after(pe, klo_w, NP * l + p + 1)
                    if l == 1:
                        pe.wait_ge(frow_in[s], 32 * (h + 1))
                for i in range(HB):
                    if l == 0:
                        after(pe, wgt_w, G + i - 3)
                        n = SPAN[i]
                        passes(Z[i][:, 0:n], b["k_hi"][r, s, i * P:(i + 1) * P], b["k_lo"][r, s, i * P:(i + 1) * P],
                               b["q_hi"][r, s, i * P:S], b["q_lo"][r, s, i * P:S], True, False)
                        mm(Z[i][:, 0:P], ident_r[:, :], maskS_r[:, :], False, True).then_inc(z_sum, 1)
                    else:
                        after(pe, plo_w, 8 * NP + G + i - 3)
                        n = P * (i + 1)
                        passes(Z[i][:, 0:n], b["q_hi"][r, s, i * P:(i + 1) * P], b["q_lo"][r, s, i * P:(i + 1) * P],
                               b["k_hi"][r, s, 0:n], b["k_lo"][r, s, 0:n], True, False)
                        mm(Z[i][:, 0:n], ones_r[32 * hb:32 * hb + 2, :], frow[32 * hb:32 * hb + 2, s, 0:n], False, False)
                        mm(Z[i][:, n - P:n], ident_r[:, :], maskF_r[:, :], False, True).then_inc(z_sum, 1)

            def middle(l, p, hb):
                G = 8 * p + 4 * hb
                if l == 0:
                    after(pe, softlo_w, G + HB)
                    for i in range(HB):
                        for j in range(i, HB):
                            w = negtri_r if i == j else negones_r
                            dst = Z[i][:, P * (j - i):SPAN[i]]
                            o = slice(OFF[j], OFF[j] + SPAN[j])
                            mm(dst, w[:, :], soft_hi[:, o], False, False)
                            last = mm(dst, w[:, :], soft_lo[:, o], False, j == HB - 1)
                        last.then_inc(r_sum, 1)
                else:
                    after(pe, p_norm, G + HB)
                    for j in range(HB):
                        for i in range(j, HB):
                            o = P * (i * (i + 1) // 2 + j)
                            last = nc.tensor.transpose(Z[j][:, P * (i - j):P * (i - j + 1)], prob[:, o:o + P],
                                                       ident[:, :])
                        last.then_inc(r_sum, 1)

            def weigh(l, p, s, hb):
                b = att[l]
                G = 8 * p + 4 * hb
                if hb == 0:
                    after(pe, vlo_w, NP * l + p + 1)
                    if l == 1:
                        pe.wait_ge(f_y, 1)
                after(pe, olo_w, 2 * NP * l + 2 * p + hb - 1)
                for i in range(HB):
                    after(pe, plo_w, 8 * NP * l + G + i + 1)
                    o = slice(i * P, (i + 1) * P)
                    passes(OB[hb][:, i * P:S], b["v_hi"][:, s, o], b["v_lo"][:, s, o],
                           b["p_hi"][:, b["p_at"][i]], b["p_lo"][:, b["p_at"][i]], i == 0, i == HB - 1
                           ).then_inc(pv, 1)

            def project_q(l, p, ready=None):
                after(pe, vT_w, NP * l + p)
                if l == 0:
                    after(pe, mod_w, p + 3)
                unit(PA[:, :], (U_L * l, p), h_hi, h_lo, ready=ready)

            def sum_q(l, p):
                if l == 1:
                    after(pe, qk_sq, 2 * p + 1)
                    after(pe, vlo_w, NP * l + p)
                    mm(PB[:, :], headones[:, :], sq[:, 0, :], True, True).then_inc(qk_sum, 1)

            def project_k(l, p):
                if l == 0:
                    after(pe, vlo_w, p)
                    unit(PB[:, :], (U_L * l + 1, p), h_hi, h_lo)
                else:
                    after(pe, qk_ln, 2 * p + 1)
                    unit(PB[:, :], (U_L * l + 1, p), hk_hi, hk_lo)

            def sum_k(l, p):
                if l == 1:
                    after(pe, qk_sq, 2 * p + 2)
                    after(pe, qk_n, 2 * p + 1)
                    mm(PA[:, :], headones[:, :], sq[:, 0, :], True, True).then_inc(qk_sum, 1)

            def project_v(l, p):
                if l == 0:
                    after(pe, qlo_w, p + 1)
                    unit(PA[:, :], (U_L * l + 2, p), h_hi, h_lo)
                else:
                    after(pe, qk_ln, 2 * p + 2)
                    unit(PA[:, :], (U_L * l + 2, p), hk_hi, hk_lo)

            def transpose_v(l, p):
                after(pe, vT_w, NP * l + p + 1)
                if l == 0:
                    after(pe, klo_w, p + 1)
                else:
                    after(pe, qk_n, 2 * p + 2)
                for i in range(TB):
                    last = nc.tensor.transpose(PB[:, i * P:(i + 1) * P], sq[:, 1, i * P:(i + 1) * P], ident[:, :])
                last.then_inc(v_T, 1)

            def step(l, p, s, h, first=False, last=False):
                scores(l, p, s, h, 0)
                if not first:
                    weigh(l, p - 1, 1 - s, 1)
                if not last:
                    project_q(l, p + 1)
                middle(l, p, 0)
                if not last:
                    sum_q(l, p + 1)
                    project_k(l, p + 1)
                scores(l, p, s, h, 1)
                weigh(l, p, s, 0)
                if not last:
                    sum_k(l, p + 1)
                    project_v(l, p + 1)
                middle(l, p, 1)
                if not last:
                    transpose_v(l, p + 1)
                if l == 0:
                    modulation(p + 4, PA)

            pe.wait_ge(consts, N_CONSTS)
            pe.wait_ge(rows_in, 16 * 14)
            nc.tensor.transpose(Z[0][:, 0:NM], rows1[0:NM, :], ident[0:NM, 0:NM]).then_inc(rows_T, 1)
            nc.tensor.transpose(Z[1][:, 0:NG], rows2[0:NG, :], ident[0:NG, 0:NG]).then_inc(rows_T, 1)
            pe.wait_ge(x_in, 16)
            for t in range(KT):
                after(pe, x_ready, t - 1)
                for b in range(TB):
                    last = nc.tensor.transpose(OB[t % 2][:, b * P:(b + 1) * P], x_nat[:, b, t * P:(t + 1) * P],
                                               ident[:, :])
                last.then_inc(x_T, 1)
            for t in range(KT):
                square_sum(0, t, t % 2, t == 0, t == KT - 1)
            for ch in range(4):
                modulation(ch, PB)

            for l in range(2):
                base = U_L * l
                hb0, hb1 = HBASE[2 * l], HBASE[2 * l + 1]

                if l == 1:
                    pe.wait_ge(wfs_lo, 1)
                    for k in range(KT):
                        pe.wait_ge(hlo_w, hb0 + KT + k + 1)
                        last = passes(OB[0][:, :], wf_hi[:, k, :], wf_lo[:, k, :], hk_hi[:, k, :], hk_lo[:, k, :],
                                      k == 0, k == KT - 1)
                    last.then_inc(f_sum, 1)
                project_q(l, 0, ready=lambda k: pe.wait_ge(hlo_w, hb0 + k + 1))
                sum_q(l, 0)
                project_k(l, 0)
                sum_k(l, 0)
                project_v(l, 0)
                transpose_v(l, 0)
                step(l, 0, 0, 0, first=True)
                with pe.Fori(0, NP // 2 - 1) as i:
                    step(l, 2 * i + 1, 1, i)
                    step(l, 2 * i + 2, 0, i + 1)
                step(l, NP - 1, 1, NP // 2 - 1, last=True)
                weigh(l, NP - 1, 1, 1)

                o_hi, o_lo = att[l]["o_hi"], att[l]["o_lo"]
                for t in range(KT):
                    if t >= 3:
                        pe.wait_ge(x_ready, KT * (2 * l + 1) + t - 2)
                    unit(Z[t % 3][:, :], (base + U_O + t, 0), o_hi, o_lo,
                         ready=(lambda k: pe.wait_ge(olo_w, 2 * NP * l + 2 * (k + 1))) if t == 0 else None)
                    if t > 0:
                        square_sum(2 * l + 1, t - 1, (t - 1) % 2, t == 1)
                    if l == 0 and t in (3, 6):
                        modulation(12 + t // 6, PB)
                square_sum(2 * l + 1, KT - 1, (KT - 1) % 2, last=True)

                def feed(u, e, r, free, ready=None, ch=None):
                    if free is not None:
                        after(pe, m_w, free)
                    unit(bank[2 + 2 * r][:, :], (u, e), h_hi, h_lo, ready=ready)
                    if ch is not None:
                        modulation(ch, PB)
                    unit(bank[3 + 2 * r][:, :], (u + 1, e), h_hi, h_lo)

                def feed3(i):
                    for r in range(3):
                        feed(base + U_F + 2 + 2 * r, 2 * i, r, FT * l + 3 * i + max(r - 1, 0),
                             ch=i + ADA_F if l == 0 and r == 2 else None)
                feed(base + U_F, 0, 2, None, ready=lambda k: pe.wait_ge(hlo_w, hb1 + k + 1))
                feed3(0)
                with pe.Fori(1, FT // 3) as i:
                    feed3(i)

                m_hi, m_lo = mid[l]

                def down(t, s, first=False):
                    if not first:
                        pe.wait_ge(x_ready, KT * (2 * l + 2) + t - 1)
                    for j, (k0, k1) in enumerate(((0, 8), (8, 16), (16, FT))):
                        if l == 0 and j == 1 and not (first and s == 0):
                            modulation(t + ADA_D - 1, PB)
                        unit(bank[2 + s][:, :], (base + U_D + j, t), m_hi, m_lo, k1 - k0, k0, j == 0, j == 2,
                             ready=(lambda k: pe.wait_ge(mlo_w, FT * l + k + 1)) if first else None)

                down(0, 0, True)
                down(1, 1, True)
                if l == 0:
                    square_sum(2, 0, 0, first=True)
                with pe.Fori(1, KT // 2) as i:
                    down(2 * i, 0)
                    if l == 0:
                        square_sum(2, 2 * i - 1, 1)
                    down(2 * i + 1, 1)
                    if l == 0:
                        square_sum(2, 2 * i, 0)
                if l == 0:
                    square_sum(2, KT - 1, 1, last=True)

            pe.wait_ge(x_ready, KT * 5)
            for k in range(2 * TB):
                after(pe, y_w, k - 3)
                for j in range(4):
                    t = 4 * (k % 2) + j
                    last = nc.tensor.transpose(Z[k % 4][:, j * P:(j + 1) * P], xT[:, t, (k // 2) * P:(k // 2 + 1) * P],
                                               ident[:, :])
                last.then_inc(y_T, 1)

        @block.scalar
        def _(act):
            A = nc.scalar.activation

            def exp_ln_tables():
                act.add_instruction(mybir.InstLoadActFuncSet(name=nc.get_next_instruction_name(),
                                                             act_func_set_id=EXP_LN_SET, ins=[], outs=[]))

            def split(u):
                b, e = u
                s = b % SLOTS
                after(act, unit_used, b - 2 + 3 * e)
                after(act, raw_in[s], 16 * (b // SLOTS + 1 + e))
                nc.scalar.copy(w_hi[:, s, :, :], raw[:, s, :, :]).then_inc(split_hi, 1)

            def square(n, t, s):
                after(act, x_ready, KT * n + t + 1)
                after(act, sq_sum, KT * n + t - 1)
                A(sq[:, s, :], xT[:, t, :], ACT.Square).then_inc(sq_w, 1)

            def norm(n):
                act.wait_ge(sq_sum, KT * (n + 1))
                A(rstd[:, :], PA[:, :], ACT.Ln, bias=epsc[:, 0:1], scale=1.0 / D).then_inc(rs_ln, 1)
                act.wait_ge(rs_ln, n + 1)
                A(rstd[:, :], rstd[:, :], ACT.Exp, scale=-0.5).then_inc(rs_w, 1)
                shifts = {0: [M_SHA], 1: [M_SHF], 2: [M_L1 + M_SHA, M_KVSH], 3: [M_L1 + M_SHF]}[n]
                for m, sh in enumerate(shifts):
                    for t in range(KT):
                        act.wait_ge(ht_w, HBASE[n] + KT * m + t + 1)
                        A((hk_hi if m else h_hi)[:, t, :], tmp[:, t % 2, :], ACT.Identity,
                          bias=mods[:, sh + t:sh + t + 1]).then_inc(hhi_w, 1)

            def chain(l, p, hb):
                G = 8 * p + 4 * hb
                if l == 0:
                    for i in range(HB):
                        o = slice(OFF[i], OFF[i] + SPAN[i])
                        after(act, z_sum, G + i + 1)
                        after(act, softlo_w, G + i - 7)
                        A(soft[:, hb, o], Z[i][:, 0:SPAN[i]], ACT.Abs).then_inc(z_abs, 1)
                    for i in range(HB):
                        o = slice(OFF[i], OFF[i] + SPAN[i])
                        after(act, z_abs, G + i + 1)
                        A(soft[:, hb, o], soft[:, hb, o], ACT.Exp, scale=-1.0).then_inc(z_exp, 1)
                    for i in range(HB):
                        o = slice(OFF[i], OFF[i] + SPAN[i])
                        after(act, z_exp, G + i + 1)
                        A(soft[:, hb, o], soft[:, hb, o], ACT.Ln, bias=1.0).then_inc(z_ln, 1)
                else:
                    after(act, negmax_w, 2 * p + hb + 1)
                    after(act, r_sum, 8 * NP + G)
                    for i in range(HB):
                        o = P * (i * (i + 1) // 2)
                        A(prob[:, o:o + P * (i + 1)], Z[i][:, 0:P * (i + 1)], ACT.Exp, bias=stat[:, 1, i:i + 1],
                          accum_out=stat[:, 2, i:i + 1]).then_inc(p_exp, 1)

            def weights(l, p, hb):
                G = 8 * p + 4 * hb
                for i in range(HB):
                    after(act, r_sum, 8 * NP * l + G + i + 1)
                    if l == 0:
                        after(act, plo_w, G + i - 1)
                        A(wgt[:, i % 2, 0:SPAN[i]], Z[i][:, 0:SPAN[i]], ACT.Exp).then_inc(wgt_w, 1)
                    else:
                        after(act, pv, 8 * NP + G + i - 3)
                        nc.scalar.copy(att[1]["p_hi"][:, att[1]["p_at"][i]], Z[i][:, 0:SPAN[i]]).then_inc(phi_w, 1)

            def out_hi(l, p, hb):
                r = slice(DH * hb, DH * hb + DH)
                after(act, pv, 8 * NP * l + 8 * p + 4 * hb + HB)
                dst = att[l]["o_hi"]
                dst = dst[r, p, :] if isinstance(p, int) else dst[r, DSL(p, 1), :].rearrange("q a s -> q (a s)")
                nc.scalar.copy(dst, OB[hb][r, :]).then_inc(ohi_w, 1)

            def q_first(l, p, s):
                after(act, unit_used, U_L * l + 3 * p + 1)
                if l == 0:
                    A(att[0]["q_hi"][:, s, :], PA[:, :], ACT.Copy, scale=DH ** -0.5).then_inc(qhi_w, 1)
                else:
                    A(sq[:, 0, :], PA[:, :], ACT.Square).then_inc(qk_sq, 1)

            def k_first(l, p, s):
                after(act, unit_used, U_L * l + 3 * p + 2)
                if l == 0:
                    nc.scalar.copy(att[0]["k_hi"][:, s, :], PB[:, :]).then_inc(khi_w, 1)
                else:
                    A(sq[:, 0, :], PB[:, :], ACT.Square).then_inc(qk_sq, 1)

            def head_norm(l, p, s, j):
                if l == 0:
                    return
                n = 2 * p + j + 1
                after(act, qk_sum, n)
                A(rstd[:, :], (PA if j else PB)[:, :], ACT.Ln, bias=epsc[:, 0:1], scale=1.0 / DH).then_inc(qk_ln, 1)
                after(act, qk_ln, n)
                A(rstd[:, :], rstd[:, :], ACT.Exp, scale=-0.5).then_inc(qk_rs, 1)
                after(act, qk_n, n)
                nc.scalar.copy(att[1]["k_hi" if j else "q_hi"][:, s, :], tmp[:, j, :]).then_inc(khi_w if j else qhi_w, 1)

            def v_rows(l, p):
                after(act, unit_used, U_L * l + 3 * p + 3)
                nc.scalar.copy(sq[:, 1, :], PA[:, :]).then_inc(vT_w, 1)

            def v_last(l, p, s):
                after(act, v_T, NP * l + p + 1)
                nc.scalar.copy(att[l]["v_hi"][:, s, :], PB[:, :]).then_inc(vhi_w, 1)

            def step(l, p, s, first=False, last=False, more=True):
                base = U_L * l
                chain(l, p, 0)
                if not first:
                    out_hi(l, p - 1, 1)
                if not last:
                    q_first(l, p + 1, 1 - s)
                    split((base, p + 2))
                weights(l, p, 0)
                if not last:
                    head_norm(l, p + 1, 1 - s, 0)
                    k_first(l, p + 1, 1 - s)
                    split((base + 1, p + 2))
                chain(l, p, 1)
                out_hi(l, p, 0)
                if not last:
                    head_norm(l, p + 1, 1 - s, 1)
                    v_rows(l, p + 1)
                    split((base + 2, p + 2))
                weights(l, p, 1)
                if not last:
                    v_last(l, p + 1, 1 - s)

            exp_ln_tables()
            act.wait_ge(cols_w, 2)
            A(cact[:, 0, :], gains[:, G_C:G_C + KT], ACT.Exp, scale=-1.0).then_inc(silu_c, 1)
            for j in range(3):
                split((j, 0))
            for t in range(KT):
                square(0, t, t % 2)

            for l in range(2):
                base = U_L * l
                if l == 1:
                    exp_ln_tables()
                norm(2 * l)
                if l == 1:
                    act.wait_ge(wf_in, 16)
                    act.wait_ge(wf_zero, 2)
                    nc.scalar.copy(wf_hi[:, :, 0:H], wf_raw[:, :, :]).then_inc(wfs_hi, 1)
                    act.wait_ge(f_y, 1)
                    A(sq[0:H, 0, :], tmp[0:H, 0, :], ACT.Abs).then_inc(f_act, 1)
                    act.wait_ge(f_act, 1)
                    A(sq[0:H, 0, :], sq[0:H, 0, :], ACT.Exp, scale=-1.0).then_inc(f_act, 1)
                    act.wait_ge(f_act, 2)
                    A(sq[0:H, 0, :], sq[0:H, 0, :], ACT.Ln, bias=1.0).then_inc(f_act, 1)
                    act.wait_ge(f_dve, 2)
                    nc.scalar.copy(tmp[0:H, 0, :].bitcast(F32R), rstd[0:H, :]).then_inc(f_act, 1)
                q_first(l, 0, 0)
                split((base, 1))
                if l == 1:
                    act.wait_ge(f_split, 1)
                head_norm(l, 0, 0, 0)
                k_first(l, 0, 0)
                split((base + 1, 1))
                head_norm(l, 0, 0, 1)
                v_rows(l, 0)
                split((base + 2, 1))
                v_last(l, 0, 0)
                step(l, 0, 0, first=True)
                with act.Fori(0, NP // 2 - 1) as i:
                    step(l, 2 * i + 1, 1)
                    step(l, 2 * i + 2, 0)
                step(l, NP - 1, 1, last=True)
                out_hi(l, NP - 1, 1)

                for t in range(KT):
                    split((base + U_O + 3 + t, 0))
                    square(2 * l + 1, t, t % 2)
                norm(2 * l + 1)

                def feed(u, e, n, r):
                    b = (tmp[:, 0, :], tmp[:, 1, :], sq[:, 0, :])[r]
                    after(act, unit_used, u + 1 + 3 * e)
                    after(act, mlo_w, n - 2)
                    A(b, bank[2 + 2 * r][:, :], ACT.Silu).then_inc(silu_w, 1)
                    split((u + 3, e))
                    after(act, m_w, n + 1)
                    f = n - FT * l
                    dst = mid[l][0]
                    dst = dst[:, f, :] if isinstance(f, int) else dst[:, DSL(f, 1), :].rearrange("q a s -> q (a s)")
                    nc.scalar.copy(dst, b).then_inc(mhi_w, 1)
                    split((u + 4, e))

                def feed3(i):
                    for r in range(3):
                        feed(base + U_F + 2 + 2 * r, 2 * i, FT * l + 3 * i + 1 + r, r)
                feed(base + U_F, 0, FT * l, 2)
                feed3(0)
                with act.Fori(1, FT // 3) as i:
                    feed3(i)

                def down(t, s, more=3):
                    for j in range(more):
                        split((base + U_D + 3 + j, t))
                    if l == 0:
                        after(act, x_ready, KT * 2 + t + 1)
                        after(act, sq_sum, KT * 2 + t - 1)
                        src = xT[:, t, :] if isinstance(t, int) else xT[:, DSL(t, 1), :].rearrange("q a s -> q (a s)")
                        A(sq[:, s, :], src, ACT.Square).then_inc(sq_w, 1)
                with act.Fori(0, KT // 2 - 1) as i:
                    down(2 * i, 0)
                    down(2 * i + 1, 1)
                down(KT - 2, 0)
                down(KT - 1, 1, more=3 if l == 0 else 0)

        @block.vector
        def _(dve):
            V = nc.vector

            def split(u):
                b, e = u
                s = b % SLOTS
                after(dve, split_hi, b + 1 + 3 * e)
                V.tensor_tensor(w_lo[:, s, :, :], raw[:, s, :, :], w_hi[:, s, :, :].bitcast(F32),
                                ALU.subtract).then_inc(split_lo, 1)

            def lo(dst, v, hi):
                return V.tensor_tensor(dst, v, hi.bitcast(F32), ALU.subtract)

            def ada_chunk(ch):
                for o in range(8):
                    r, k = o // 2, o % 2
                    if k == 0:
                        after(dve, ada_in[r], 16 * ch + 16)
                    cc = cact[:, 1, o:o + 1]
                    if o == 0:
                        after(dve, mod_sum, ch)
                        V.tensor_scalar(acc[:, :], ada[:, r, k, :], cc, None, ALU.mult).then_inc(acc_step, 1)
                    else:
                        after(dve, acc_step, 8 * ch + o)
                        V.scalar_tensor_tensor(acc[:, :], ada[:, r, k, :], cc, acc[:, :], ALU.mult,
                                               ALU.add).then_inc(acc_step, 1)

            def mods_out(ch, b):
                after(dve, mod_sum, ch + 1)
                o = slice(4 * ch, 4 * ch + 4) if isinstance(ch, int) else DSL(4 * ch, 4)
                V.tensor_tensor(mods[:, o], b[:, 0:4], mod_bias[:, o], ALU.add).then_inc(mod_w, 1)

            def gain(j, sc, g):
                V.scalar_tensor_tensor(amod[:, j, :], mods[:, sc:sc + KT], 1.0, gains[:, g:g + KT], ALU.add,
                                       ALU.mult).then_inc(amod_w, 1)

            def norm(n):
                sets = {0: [(0, M_SHA, h_hi, h_lo)], 1: [(1, M_SHF, h_hi, h_lo)],
                        2: [(2, M_L1 + M_SHA, h_hi, h_lo), (3, M_KVSH, hk_hi, hk_lo)],
                        3: [(4, M_L1 + M_SHF, h_hi, h_lo)]}[n]
                dve.wait_ge(rs_w, n + 1)

                def modulated(m, t):
                    if KT * m + t >= 2:
                        dve.wait_ge(hlo_w, HBASE[n] + KT * m + t - 1)
                    V.scalar_tensor_tensor(tmp[:, t % 2, :], xT[:, t, :], amod[:, sets[m][0], t:t + 1], rstd[:, :],
                                           ALU.mult, ALU.mult).then_inc(ht_w, 1)

                def low(m, t):
                    _, sh, hi, lo_ = sets[m]
                    dve.wait_ge(hhi_w, HBASE[n] + KT * m + t + 1)
                    V.scalar_tensor_tensor(lo_[:, t, :], tmp[:, t % 2, :], mods[:, sh + t:sh + t + 1],
                                           hi[:, t, :].bitcast(F32), ALU.add, ALU.subtract).then_inc(hlo_w, 1)
                order = [(m, t) for m in range(len(sets)) for t in range(KT)]
                modulated(*order[0])
                for a, b in zip(order, order[1:] + [None]):
                    if b:
                        modulated(*b)
                    low(*a)

            def add_x(stage, t, src, unit_n, g):
                after(dve, unit_used, unit_n)
                if isinstance(t, int):
                    d, gc = xT[:, t, :], mods[:, g + t:g + t + 1]
                else:
                    d, gc = xT[:, DSL(t, 1), :].rearrange("q a s -> q (a s)"), mods[:, DSL(t + g, 1)]
                V.scalar_tensor_tensor(d, src, gc, d, ALU.mult, ALU.add).then_inc(x_ready, 1)

            def chain(l, p, hb):
                G = 8 * p + 4 * hb
                if l == 0:
                    for i in range(HB):
                        o = slice(OFF[i], OFF[i] + SPAN[i])
                        after(dve, z_ln, G + i + 1)
                        V.scalar_tensor_tensor(soft[:, hb, o], Z[i][:, 0:SPAN[i]], 0.0, soft[:, hb, o], ALU.max,
                                               ALU.add).then_inc(soft_w, 1)
                    for i in range(HB):
                        o = slice(OFF[i], OFF[i] + SPAN[i])
                        after(dve, softhi_w, G + i + 1)
                        lo(soft_lo[:, o], soft[:, hb, o], soft_hi[:, o]).then_inc(softlo_w, 1)
                else:
                    for i in range(HB):
                        after(dve, z_sum, 8 * NP + G + i + 1)
                        V.reduce_max(stat[:, 0, i:i + 1], Z[i][:, 0:P * (i + 1)], AX.X).then_inc(max_w, 1)
                    after(dve, max_w, G + HB)
                    V.tensor_scalar(stat[:, 1, :], stat[:, 0, :], -1.0, None, ALU.mult).then_inc(negmax_w, 1)
                    after(dve, p_exp, G + HB)
                    V.reciprocal(stat[:, 3, :], stat[:, 2, :]).then_inc(inv_w, 1)
                    after(dve, inv_w, 2 * p + hb + 1)
                    for i in range(HB):
                        o = P * (i * (i + 1) // 2)
                        V.tensor_scalar(prob[:, o:o + P * (i + 1)], prob[:, o:o + P * (i + 1)], stat[:, 3, i:i + 1],
                                        None, ALU.mult).then_inc(p_norm, 1)

            def weights(l, p, hb):
                G = 8 * p + 4 * hb
                b = att[l]
                for i in range(HB):
                    after(dve, phi_w if l else whi_w, G + i + 1)
                    src = Z[i][:, 0:SPAN[i]] if l else wgt[:, i % 2, 0:SPAN[i]]
                    lo(b["p_lo"][:, b["p_at"][i]], src, b["p_hi"][:, b["p_at"][i]]).then_inc(plo_w, 1)

            def out_lo(l, p, hb):
                r = slice(DH * hb, DH * hb + DH)
                after(dve, ohi_w, 2 * NP * l + 2 * p + hb + 1)
                hi, lo_ = att[l]["o_hi"], att[l]["o_lo"]
                if isinstance(p, int):
                    hi, lo_ = hi[r, p, :], lo_[r, p, :]
                else:
                    hi, lo_ = (t[r, DSL(p, 1), :].rearrange("q a s -> q (a s)") for t in (hi, lo_))
                lo(lo_, OB[hb][r, :], hi).then_inc(olo_w, 1)

            def q_last(l, p, s):
                b = att[l]
                if l == 0:
                    after(dve, qhi_w, p + 1)
                    V.scalar_tensor_tensor(b["q_lo"][:, s, :], PA[:, :], DH ** -0.5, b["q_hi"][:, s, :].bitcast(F32),
                                           ALU.mult, ALU.subtract).then_inc(qlo_w, 1)
                else:
                    after(dve, qk_rs, 2 * p + 1)
                    V.scalar_tensor_tensor(tmp[:, 0, :], PA[:, :], gains[:, G_Q:G_Q + 1], rstd[:, :], ALU.mult,
                                           ALU.mult).then_inc(qk_n, 1)
                    after(dve, qhi_w, NP + p + 1)
                    lo(b["q_lo"][:, s, :], tmp[:, 0, :], b["q_hi"][:, s, :]).then_inc(qlo_w, 1)

            def k_last(l, p, s):
                b = att[l]
                if l == 0:
                    after(dve, khi_w, p + 1)
                    lo(b["k_lo"][:, s, :], PB[:, :], b["k_hi"][:, s, :]).then_inc(klo_w, 1)
                else:
                    after(dve, qk_rs, 2 * p + 2)
                    V.scalar_tensor_tensor(tmp[:, 1, :], PB[:, :], gains[:, G_K:G_K + 1], rstd[:, :], ALU.mult,
                                           ALU.mult).then_inc(qk_n, 1)
                    after(dve, khi_w, NP + p + 1)
                    lo(b["k_lo"][:, s, :], tmp[:, 1, :], b["k_hi"][:, s, :]).then_inc(klo_w, 1)

            def v_last(l, p, s):
                after(dve, vhi_w, NP * l + p + 1)
                lo(att[l]["v_lo"][:, s, :], PB[:, :], att[l]["v_hi"][:, s, :]).then_inc(vlo_w, 1)

            def step(l, p, s, first=False, last=False):
                base = U_L * l
                chain(l, p, 0)
                if not first:
                    out_lo(l, p - 1, 1)
                if not last:
                    if l == 0:
                        q_last(l, p + 1, 1 - s)
                    split((base, p + 2))
                weights(l, p, 0)
                if not last:
                    if l == 1:
                        q_last(l, p + 1, 1 - s)
                    else:
                        k_last(l, p + 1, 1 - s)
                    split((base + 1, p + 2))
                if l == 0:
                    ada_chunk(p + 4)
                chain(l, p, 1)
                out_lo(l, p, 0)
                if not last:
                    if l == 1:
                        k_last(l, p + 1, 1 - s)
                    split((base + 2, p + 2))
                weights(l, p, 1)
                if not last:
                    v_last(l, p + 1, 1 - s)
                if l == 0:
                    mods_out(p + 4, PA)

            dve.wait_ge(rows_T, 2)
            V.tensor_copy(mod_bias[:, :], Z[0][:, 0:NM]).then_inc(cols_w, 1)
            V.tensor_copy(gains[:, :], Z[1][:, 0:NG]).then_inc(cols_w, 1)
            dve.wait_ge(silu_c, 1)
            dve.wait_ge(cols_w, 2)
            V.tensor_scalar(cact[:, 0, :], cact[:, 0, :], 1.0, None, ALU.add).then_inc(silu_c, 1)
            dve.wait_ge(silu_c, 2)
            V.reciprocal(cact[:, 0, :], cact[:, 0, :]).then_inc(silu_c, 1)
            dve.wait_ge(silu_c, 3)
            V.tensor_tensor(cact[:, 1, :], cact[:, 0, :], gains[:, G_C:G_C + KT], ALU.mult).then_inc(silu_c, 1)
            V.tensor_scalar(gains[:, G_Q:G_Q + 1], gains[:, G_Q:G_Q + 1], DH ** -0.5, None, ALU.mult).then_inc(silu_c, 1)
            for t in range(KT):
                dve.wait_ge(x_T, t + 1)
                V.tensor_copy(xT[:, t, :], OB[t % 2][:, :]).then_inc(x_ready, 1)
            dve.wait_ge(silu_c, 5)
            for ch in range(4):
                ada_chunk(ch)
                mods_out(ch, PB)
            for j in range(3):
                split((j, 0))
            dve.wait_ge(mod_w, 4)
            gain(0, M_SCA, G_ATT)
            dve.wait_ge(amod_w, 1)

            for l in range(2):
                base = U_L * l
                norm(2 * l)
                if l == 1:
                    dve.wait_ge(wfs_hi, 1)
                    lo(wf_lo[:, :, 0:H], wf_raw[:, :, :], wf_hi[:, :, 0:H]).then_inc(wfs_lo, 1)
                    dve.wait_ge(f_sum, 1)
                    V.tensor_scalar(tmp[0:H, 0, :], OB[0][0:H, :], gains[0:H, G_BF:G_BF + 1], None,
                                    ALU.add).then_inc(f_y, 1)
                    dve.wait_ge(f_act, 1)
                    V.tensor_scalar(tmp[0:H, 0, :], tmp[0:H, 0, :], -1.0, 0.0, ALU.mult, ALU.max).then_inc(f_dve, 1)
                    dve.wait_ge(f_act, 3)
                    dve.wait_ge(f_dve, 1)
                    V.tensor_tensor_scan(rstd[0:H, :], tmp[0:H, 0, :], sq[0:H, 0, :], 0.0, ALU.add,
                                         ALU.add).then_inc(f_dve, 1)
                    dve.wait_ge(f_act, 4)
                    V.tensor_tensor(tmp[0:H, 1, :].bitcast(F32R), rstd[0:H, :], tmp[0:H, 0, :],
                                    ALU.subtract).then_inc(f_split, 1)
                if l == 0:
                    q_last(l, 0, 0)
                split((base, 1))
                if l == 1:
                    dve.wait_ge(fcum_out, 32)
                    q_last(l, 0, 0)
                k_first = l == 0
                if k_first:
                    k_last(l, 0, 0)
                split((base + 1, 1))
                if not k_first:
                    k_last(l, 0, 0)
                split((base + 2, 1))
                v_last(l, 0, 0)
                step(l, 0, 0, first=True)
                with dve.Fori(0, NP // 2 - 1) as i:
                    step(l, 2 * i + 1, 1)
                    step(l, 2 * i + 2, 0)
                step(l, NP - 1, 1, last=True)
                out_lo(l, NP - 1, 1)

                ml = M_L1 * l
                for t in range(KT):
                    add_x(2 * l + 1, t, Z[t % 3][:, :], base + U_O + t + 1, ml + M_GA)
                    split((base + U_O + 3 + t, 0))
                    if l == 0 and t in (2, 5):
                        ada_chunk(12 + t // 5)
                    if l == 0 and t in (3, 6):
                        mods_out(12 + t // 6, PB)
                if l == 0:
                    gain(1, M_SCF, G_FFN)
                    dve.wait_ge(amod_w, 2)
                norm(2 * l + 1)

                def feed(u, e, n, r, ch=None):
                    b = (tmp[:, 0, :], tmp[:, 1, :], sq[:, 0, :])[r]
                    split((u + 3, e))
                    after(dve, silu_w, n + 1)
                    after(dve, unit_used, u + 2 + 3 * e)
                    V.tensor_tensor(b, b, bank[3 + 2 * r][:, :], ALU.mult).then_inc(m_w, 1)
                    split_after = (u + 4, e)
                    f = n - FT * l
                    after(dve, mhi_w, n + 1)
                    hi, lo_ = mid[l]
                    if isinstance(f, int):
                        hi, lo_ = hi[:, f, :], lo_[:, f, :]
                    else:
                        hi, lo_ = (t[:, DSL(f, 1), :].rearrange("q a s -> q (a s)") for t in (hi, lo_))
                    lo(lo_, b, hi).then_inc(mlo_w, 1)
                    split(split_after)
                    if ch is not None and r == 0:
                        ada_chunk(ch)
                    if ch is not None and r == 2:
                        mods_out(ch, PB)

                def feed3(i):
                    for r in range(3):
                        feed(base + U_F + 2 + 2 * r, 2 * i, FT * l + 3 * i + 1 + r, r,
                             i + ADA_F if l == 0 else None)
                feed(base + U_F, 0, FT * l, 2)
                feed3(0)
                with dve.Fori(1, FT // 3) as i:
                    feed3(i)

                def down(t, s, more=3, take=True, make=True):
                    for j in range(min(more, 2)):
                        split((base + U_D + 3 + j, t))
                    if l == 0 and take:
                        mods_out(t + ADA_D - 1, PB)
                    if l == 0 and make:
                        ada_chunk(t + ADA_D)
                    add_x(2 * l + 2, t, bank[2 + s][:, :], base + U_D + 3 + 3 * t, ml + M_GF)
                    if more == 3:
                        split((base + U_D + 5, t))
                down(0, 0, take=False)
                with dve.Fori(0, KT // 2 - 1) as i:
                    down(2 * i + 1, 1)
                    down(2 * i + 2, 0)
                down(KT - 1, 1, more=3 if l == 0 else 0, make=False)
                if l == 0:
                    dve.wait_ge(mod_w, ADA_N)
                    gain(2, M_L1 + M_SCA, G_ATT + KT)
                    gain(3, M_KVSC, G_KV)
                    gain(4, M_L1 + M_SCF, G_FFN + KT)
                    dve.wait_ge(amod_w, 5)

            for k in range(2 * TB):
                dve.wait_ge(y_T, k + 1)
                if k >= 4:
                    dve.wait_ge(out_done[(k // 2) % 2], 16)
                V.tensor_copy(out_nat[:, (k // 2) % 2, (k % 2) * 512:(k % 2 + 1) * 512],
                              Z[k % 4][:, :]).then_inc(y_w, 1)


_NAMES = ["x", "c", "ada_w", "ada_b", "norm_attn_g", "norm_ffn_g", "w_ffn_in", "w_ffn_down", "sb_w_qkv", "sb_w_o",
          "kv_ada_w", "kv_ada_b", "kv_norm_g", "w_kvf", "b_f", "k_norm_g", "fox_w_q", "q_norm_g", "fox_w_o"]


def kernel(**inputs):
    import numpy as np
    import concourse.bacc as bacc
    from concourse.bass_utils import run_bass_kernel_spmd

    nc = bacc.Bacc("TRN2", target_bir_lowering=False, num_devices=1)
    arrays = {n: np.ascontiguousarray(inputs[n]) for n in _NAMES}
    aps = [nc.dram_tensor(n, arrays[n].shape, F32, kind="ExternalInput").ap() for n in _NAMES]
    res = nc.dram_tensor("result", arrays["x"].shape, F32, kind="ExternalOutput").ap()
    build(nc, *aps, res)
    return run_bass_kernel_spmd(nc, [arrays], core_ids=[0]).results[0]["result"]
```

```python
from contextlib import ExitStack

import concourse.bass as bass
from concourse import mybir

F32 = mybir.dt.float32
F32R = mybir.dt.float32r
ACT = mybir.ActivationFunctionType
ALU = mybir.AluOpType
AX = mybir.AxisListType

P = 128
SLOTS = 3
EPS = 1e-6
NEG = -(2.0 ** 100)
EXP_LN_SET = 6
N_CONSTS = 20


def after(eng, sem, n):
    if not isinstance(n, int) or n > 0:
        eng.wait_ge(sem, n)


def build(nc, x, c, ada_w, ada_b, norm_attn_g, norm_ffn_g, w_ffn_in, w_ffn_down, sb_w_qkv, sb_w_o,
          kv_ada_w, kv_ada_b, kv_norm_g, w_kvf, b_f, k_norm_g, fox_w_q, q_norm_g, fox_w_o, out):
    _, S, D = x.shape
    FF = w_ffn_down.shape[1]
    H = b_f.shape[0]
    DH = D // H
    KT = D // P
    FT = FF // P
    TB = S // P
    NP = H // 2
    SPAN = [S - P * i for i in range(TB)]
    OFF = [sum(SPAN[:i]) for i in range(TB)]
    PK = sum(SPAN)
    AT = [slice(o, o + n) for o, n in zip(OFF, SPAN)]
    HB = 4
    U_O, U_F, U_D, U_L = 3 * NP, 3 * NP + KT, 3 * NP + KT + 2 * FT, 3 * NP + KT + 2 * FT + 3 * KT
    CH = 512
    M_SHA, M_SCA, M_GA, M_SHF, M_SCF, M_GF = [KT * i for i in range(6)]
    M_KVSH, M_KVSC, M_L1 = 6 * KT, 7 * KT, 8 * KT
    NM = 14 * KT
    G_ATT, G_FFN, G_KV, G_C, G_K, G_Q, G_BF = 0, 2 * KT, 4 * KT, 5 * KT, 6 * KT, 6 * KT + 1, 6 * KT + 2
    NG = 6 * KT + 3
    ADA_F = 4 + NP + 2
    ADA_D = ADA_F + FT // 3
    ADA_N = NM // (CH // P)
    assert ADA_D + KT - 1 == ADA_N
    HBASE = [0, KT, 2 * KT, 4 * KT]

    with ExitStack() as ctx:
        def sem(name):
            return ctx.enter_context(nc.semaphore(name))

        def sb(scope, name, shape, dt=F32):
            return scope.enter_context(nc.sbuf_tensor(name, shape, dt))

        bank = [ctx.enter_context(nc.psum_tensor(f"bank{i}", [P, 512], F32)) for i in range(8)]
        PA, PB = bank[0], bank[1]
        OB = bank[2:4]
        Z = bank[4:8]
        MIX_BANK = [PA, PB, Z[2], Z[0], Z[1], Z[2], Z[0], Z[1]]

        xT = sb(ctx, "xT", [P, KT, S])
        h_hi = sb(ctx, "h_hi", [P, KT, S], F32R)
        h_lo = sb(ctx, "h_lo", [P, KT, S], F32R)
        raw = sb(ctx, "raw", [P, SLOTS, 8, P])
        w_hi = sb(ctx, "w_hi", [P, SLOTS, 8, P], F32R)
        w_lo = sb(ctx, "w_lo", [P, SLOTS, 8, P], F32R)
        sq = sb(ctx, "sq", [P, 2, S])
        tmp = sb(ctx, "tmp", [P, 2, S])
        rstd = sb(ctx, "rstd", [P, S])
        ident = sb(ctx, "ident", [P, P])
        ones = sb(ctx, "ones", [P, P])
        headones = sb(ctx, "headones", [P, P])
        build_tmp = sb(ctx, "build_tmp", [P, P])
        ident_r = sb(ctx, "ident_r", [P, P], F32R)
        ones_r = sb(ctx, "ones_r", [P, P], F32R)
        negones_r = sb(ctx, "negones_r", [P, P], F32R)
        negtri_r = sb(ctx, "negtri_r", [P, P], F32R)
        maskS_r = sb(ctx, "maskS_r", [P, P], F32R)
        maskF_r = sb(ctx, "maskF_r", [P, P], F32R)
        mods = sb(ctx, "mods", [P, NM])
        mod_bias = sb(ctx, "mod_bias", [P, NM])
        gains = sb(ctx, "gains", [P, NG])
        amod = sb(ctx, "amod", [P, 5, KT])
        cact = sb(ctx, "cact", [P, 2, KT])
        epsc = sb(ctx, "epsc", [P, 1])
        stat = sb(ctx, "stat", [P, 4, 4])
        fcum_dram = nc.dram_tensor("fcum_scratch", [2, H, S], F32, kind="Internal").ap()

        l0 = ExitStack()
        ada = sb(l0, "ada", [P, 4, 2, CH])
        acc = sb(l0, "acc", [P, CH])
        ACC = [acc[:, :], tmp[:, 0, :], tmp[:, 1, :], acc[:, :]]
        start_scope = ExitStack()
        x_nat = sb(start_scope, "x_nat", [P, TB, D])
        rows1 = sb(start_scope, "rows1", [P, P])
        rows2 = sb(start_scope, "rows2", [P, P])
        ada_first = sb(start_scope, "ada_first", [P, 4, KT, CH])
        start_scope.close()
        a0 = ExitStack()
        att = [dict(), dict()]

        def attention_buffers(scope, l):
            b = att[l]
            b["o_hi"] = sb(scope, f"o_hi{l}", [P, NP, S], F32R)
            b["o_lo"] = sb(scope, f"o_lo{l}", [P, NP, S], F32R)
            for n in "qkv":
                b[n + "_hi"] = sb(scope, f"{n}_hi{l}", [P, 2, S], F32R)
                b[n + "_lo"] = sb(scope, f"{n}_lo{l}", [P, 2, S], F32R)
            b["p_hi"] = sb(scope, f"p_hi{l}", [P, PK], F32R)
            b["p_lo"] = sb(scope, f"p_lo{l}", [P, PK], F32R)

        attention_buffers(a0, 0)
        soft = sb(a0, "soft", [P, PK])
        soft_hi = sb(a0, "soft_hi", [P, PK], F32R)
        soft_lo = sb(a0, "soft_lo", [P, PK], F32R)
        wgt = sb(a0, "wgt", [P, PK])
        a0.close()
        f0 = ExitStack()
        mid = [dict(), dict()]
        mid[0] = (sb(f0, "mid_hi0", [P, FT, S], F32R), sb(f0, "mid_lo0", [P, FT, S], F32R))
        f0.close()
        l0.close()
        a1 = ExitStack()
        wf_scope = ExitStack()
        wf_hi = sb(wf_scope, "wf_hi", [P, KT, P], F32R)
        wf_lo = sb(wf_scope, "wf_lo", [P, KT, P], F32R)
        wf_raw = sb(wf_scope, "wf_raw", [P, KT, H])
        assert KT * (2 * P + H) <= 4 * 2 * CH
        wf_scope.close()
        attention_buffers(a1, 1)
        hk_hi = sb(a1, "hk_hi", [P, KT, S], F32R)
        hk_lo = sb(a1, "hk_lo", [P, KT, S], F32R)
        frow = sb(a1, "frow", [P, 2, S], F32R)
        prob = sb(a1, "prob", [P, PK])
        f_relu, f_soft = prob[0:H, 0:S], prob[0:H, S:2 * S]
        f_hi, f_lo = att[1]["p_hi"][0:H, 0:S], att[1]["p_lo"][0:H, 0:S]
        k_rstd = prob[:, 0:S]
        a1.close()
        f1 = ExitStack()
        mid[1] = (sb(f1, "mid_hi1", [P, FT, S], F32R), sb(f1, "mid_lo1", [P, FT, S], F32R))
        out_nat = sb(f1, "out_nat", [P, TB, D])
        f1.close()

        raw_in = [sem(f"raw_in{i}") for i in range(SLOTS)]
        ada_in = [sem(f"ada_in{i}") for i in range(4)]
        first_in = [[sem(f"first_in{i}{j}") for j in range(2)] for i in range(4)]
        x_in, rows_in, wf_in, fcum_out = (sem(n) for n in ("x_in", "rows_in", "wf_in", "fcum_out"))
        out_done = sem("out_done")
        frow_in = [sem("frow_in0"), sem("frow_in1")]
        split_hi, split_lo, unit_used = sem("split_hi"), sem("split_lo"), sem("unit_used")
        consts, rows_zero, wf_zero = sem("consts"), sem("rows_zero"), sem("wf_zero")
        rows_T, cols_w, silu_c = sem("rows_T"), sem("cols_w"), sem("silu_c")
        x_T, x_ready = sem("x_T"), sem("x_ready")
        acc_step, mod_sum, mod_w, amod_w = sem("acc_step"), sem("mod_sum"), sem("mod_w"), sem("amod_w")
        sq_w, sq_acc, sq_sum, rs_ln, rs_w = sem("sq_w"), sem("sq_acc"), sem("sq_sum"), sem("rs_ln"), sem("rs_w")
        ht_w, hhi_w, hlo_w = sem("ht_w"), sem("hhi_w"), sem("hlo_w")
        wfs_hi, wfs_lo = sem("wfs_hi"), sem("wfs_lo")
        f_sum, f_y, f_act, f_dve, f_split = sem("f_sum"), sem("f_y"), sem("f_act"), sem("f_dve"), sem("f_split")
        qhi_w, khi_w, vhi_w = sem("qhi_w"), sem("khi_w"), sem("vhi_w")
        qlo_w, klo_w, vlo_w = sem("qlo_w"), sem("klo_w"), sem("vlo_w")
        vT_w, v_T = sem("vT_w"), sem("v_T")
        qk_sq, qk_sum, qk_ln, qk_rs, qk_n = sem("qk_sq"), sem("qk_sum"), sem("qk_ln"), sem("qk_rs"), sem("qk_n")
        z_sum, z_abs, z_exp, z_ln = sem("z_sum"), sem("z_abs"), sem("z_exp"), sem("z_ln")
        soft_w, softhi_w, softlo_w = sem("soft_w"), sem("softhi_w"), sem("softlo_w")
        r_sum, phi_w, plo_w, pv = sem("r_sum"), sem("phi_w"), sem("plo_w"), sem("pv")
        max_w, negmax_w, p_exp, inv_w, p_norm = (sem(n) for n in ("max_w", "negmax_w", "p_exp", "inv_w", "p_norm"))
        ohi_w, olo_w = sem("ohi_w"), sem("olo_w")
        silu_w, m_w, mhi_w, mlo_w = sem("silu_w"), sem("m_w"), sem("mhi_w"), sem("mlo_w")
        y_T, y_w, y_last = sem("y_T"), sem("y_w"), sem("y_last")

        def ka(w):
            return w.rearrange("(k p) n -> p k n", p=P)

        WQKV = [(ka(sb_w_qkv[0]), ka(sb_w_qkv[0]), ka(sb_w_qkv[0])), (ka(fox_w_q[0]), ka(w_kvf), ka(w_kvf))]
        CQKV = [(0, D, 2 * D), (0, 0, D)]
        WO = [ka(sb_w_o[0]), ka(fox_w_o[0])]
        DSL = bass.ds
        block = ctx.enter_context(nc.Block())

        def row(v):
            return v.rearrange("(r q) -> r q", r=1)

        def rows_of(v):
            return v.rearrange("(r q) -> r q", q=P)
        ROWS = [[(rows2[G_C:G_C + KT, :], rows_of(c[0])),
                 (rows1[0:6 * KT, :], rows_of(ada_b[0])),
                 (rows1[8 * KT:14 * KT, :], rows_of(ada_b[1])),
                 (rows1[6 * KT:8 * KT, :], rows_of(kv_ada_b)),
                 (rows2[G_K:G_K + 1, 0:DH], row(k_norm_g)),
                 (rows2[G_K:G_K + 1, DH:P], row(k_norm_g))],
                [(rows2[G_ATT:G_ATT + 2 * KT, :], norm_attn_g.rearrange("l (r q) -> (l r) q", q=P)),
                 (rows2[G_FFN:G_FFN + 2 * KT, :], norm_ffn_g.rearrange("l (r q) -> (l r) q", q=P)),
                 (rows2[G_KV:G_KV + KT, :], rows_of(kv_norm_g)),
                 (rows2[G_Q:G_Q + 1, 0:DH], row(q_norm_g[0])),
                 (rows2[G_Q:G_Q + 1, DH:P], row(q_norm_g[0])),
                 (rows2[G_BF:G_BF + 1, 0:H], row(b_f))]]

        def load_rows(eng, half):
            eng.wait_ge(rows_zero, 1)
            for dst, src in ROWS[half]:
                eng.dma_start(dst, src).then_inc(rows_in, 16)

        def y_bank(t, b):
            return PA if t == KT - 1 and b >= 2 else Z[t % 4]

        def y_out(copy, t, b0, b1):
            return copy(out_nat[:, b0:b1, t * P:(t + 1) * P],
                        y_bank(t, b0)[:, b0 * P:b1 * P].rearrange("p (b q) -> p b q", q=P))

        @block.sync
        def _(sp):
            def load(u, src, nk=8):
                b, e = u
                after(sp, split_lo, b - 2 + 3 * e)
                sp.dma_start(raw[:, b % SLOTS, 0:nk, :], src).then_inc(raw_in[b % SLOTS], 16)

            load_rows(sp, 1)
            for ch in range(4):
                for h in range(2):
                    k = slice(h * KT // 2, (h + 1) * KT // 2)
                    sp.dma_start(ada_first[:, ch, k, :],
                                 ka(ada_w[0])[:, k, CH * ch:CH * (ch + 1)]).then_inc(first_in[ch][h], 16)
                if ch > 0:
                    load((ch - 1, 0), ka(sb_w_qkv[0])[:, :, (ch - 1) * D:(ch - 1) * D + P])

            for l in range(2):
                base = U_L * l

                def load_qkv(p, static):
                    for i, j in enumerate((1, 2, 0) if static and l else (0, 1, 2)):
                        u = (base + i, p)
                        load(u, WQKV[l][j][:, :, DSL(p * P + CQKV[l][j], P)] if not static else
                             WQKV[l][j][:, :, p * P + CQKV[l][j]:p * P + CQKV[l][j] + P])
                if l == 1:
                    load_qkv(0, True)
                with sp.Fori(1, NP) as p:
                    load_qkv(p, False)
                for j in range(KT):
                    load((base + U_O + j, 0), WO[l][:, :, j * P:(j + 1) * P])
                w_in, w_dn = ka(w_ffn_in[l]), ka(w_ffn_down[l])
                load((base + U_F, 0), w_in[:, :, 0:P])
                load((base + U_F + 1, 0), w_in[:, :, FF:FF + P])
                with sp.Fori(0, FT // 3) as i:
                    for r in range(3):
                        load((base + U_F + 2 + 2 * r, 2 * i), w_in[:, :, DSL((3 * i + 1 + r) * P, P)])
                        load((base + U_F + 3 + 2 * r, 2 * i), w_in[:, :, DSL((3 * i + 1 + r) * P + FF, P)])
                with sp.Fori(0, KT) as t:
                    for r, (k0, k1) in enumerate(((0, 8), (8, 16), (16, FT))):
                        load((base + U_D + r, t), w_dn[:, k0:k1, DSL(t * P, P)], k1 - k0)

            result = out[0].rearrange("(b p) d -> p b d", p=P)
            for t0, t1 in ((0, 4), (4, KT - 1), (KT - 1, KT)):
                sp.wait_ge(y_w, t1)
                if t1 == KT:
                    sp.wait_ge(y_last, 1)
                sp.dma_start(result[:, :, t0 * P:t1 * P], out_nat[:, :, t0 * P:t1 * P]).then_inc(out_done, 16)
            sp.wait_ge(out_done, 48)

        @block.gpsimd
        def _(pool):
            pool.memset(rows2[:, :], 0.0).then_inc(rows_zero, 1)
            pool.dma_start(x_nat[:, :, :], x[0].rearrange("(b p) d -> p b d", p=P)).then_inc(x_in, 16)
            pool.memset(ident[:, :], 0.0).then_inc(consts, 1)
            pool.memset(ones[:, :], 1.0).then_inc(consts, 1)
            pool.memset(headones[:, :], 0.0).then_inc(consts, 1)
            pool.memset(epsc[:, :], EPS).then_inc(consts, 1)
            pool.wait_ge(consts, 4)
            pool.affine_select(out=ident[:, :], in_=ident[:, :], compare_op=ALU.not_equal, fill=1.0,
                               base=0, pattern=[[-1, P]], channel_multiplier=1).then_inc(consts, 1)
            pool.wait_ge(consts, 5)
            pool.memset(headones[0:DH, 0:DH], 1.0).then_inc(consts, 1)
            pool.wait_ge(consts, 6)
            pool.memset(headones[DH:P, DH:P], 1.0).then_inc(consts, 1)
            pool.wait_ge(consts, 7)
            pool.tensor_copy(ident_r[:, :], ident[:, :]).then_inc(consts, 1)
            pool.tensor_copy(ones_r[:, :], ones[:, :]).then_inc(consts, 1)
            n = 9
            for dst, val, cmp, step in ((negones_r, -1.0, None, 0), (negtri_r, -1.0, ALU.is_ge, -1),
                                        (maskS_r, NEG, ALU.is_ge, -1), (maskF_r, NEG, ALU.is_gt, 1)):
                pool.memset(build_tmp[:, :], val).then_inc(consts, 1)
                n += 1
                pool.wait_ge(consts, n)
                if cmp is not None:
                    pool.affine_select(out=build_tmp[:, :], in_=build_tmp[:, :], compare_op=cmp, fill=0.0,
                                       base=0, pattern=[[step, P]], channel_multiplier=-step).then_inc(consts, 1)
                    n += 1
                    pool.wait_ge(consts, n)
                pool.tensor_copy(dst[:, :], build_tmp[:, :]).then_inc(consts, 1)
                n += 1
                pool.wait_ge(consts, n)
            assert n == N_CONSTS

            def pieces(w):
                wv = w.rearrange("(r k p) n -> r p k n", k=2, p=P)
                return [wv[r] for r in range(4)]

            def load_ada(ch, w, col):
                for r, piece in enumerate(pieces(w)):
                    pool.wait_ge(acc_step, 8 * ch - 6 + 2 * r)
                    pool.dma_start(ada[:, r, :, :], piece[:, :, col]).then_inc(ada_in[r], 16)

            pool.wait_ge(acc_step, 24)
            for r, piece in enumerate(pieces(ada_w[0])):
                pool.dma_start(ada[:, r, :, :], piece[:, :, 4 * CH:5 * CH]).then_inc(ada_in[r], 16)
            with pool.Fori(5, 12) as ch:
                load_ada(ch, ada_w[0], DSL(ch * CH, CH))
            with pool.Fori(0, 4) as ch:
                load_ada(ch + 12, kv_ada_w, DSL(ch * CH, CH))
            with pool.Fori(0, 12) as ch:
                load_ada(ch + 16, ada_w[1], DSL(ch * CH, CH))

            pool.wait_ge(acc_step, 8 * ADA_N)
            pool.dma_start(wf_raw[:, :, :], ka(w_kvf)[:, :, 2 * D:2 * D + H]).then_inc(wf_in, 16)
            pool.memset(wf_hi[:, :, :].bitcast(F32), 0.0).then_inc(wf_zero, 1)
            pool.memset(wf_lo[:, :, :].bitcast(F32), 0.0).then_inc(wf_zero, 1)
            pool.wait_ge(f_split, 1)
            pool.dma_start(fcum_dram[0], f_hi.bitcast(F32)).then_inc(fcum_out, 16)
            pool.dma_start(fcum_dram[1], f_lo.bitcast(F32)).then_inc(fcum_out, 16)
            pool.wait_ge(fcum_out, 32)

            def load_frow(s, p, static):
                for hb in range(2):
                    src = fcum_dram[:, 2 * p + hb, :] if static else \
                        fcum_dram[:, DSL(2 * p + hb, 1), :].rearrange("a b s -> a (b s)")
                    pool.dma_start(frow[32 * hb:32 * hb + 2, s, :].bitcast(F32), src).then_inc(frow_in[s], 16)
            load_frow(0, 0, True)
            load_frow(1, 1, True)
            with pool.Fori(1, NP // 2) as i:
                for s in range(2):
                    pool.wait_ge(z_sum, 8 * NP + 8 * (2 * i + s - 1))
                    load_frow(s, 2 * i + s, False)

        @block.tensor
        def _(pe):
            def mm(dst, w, m, start, stop):
                return nc.tensor.matmul(dst, w, m, start=start, stop=stop, skip_group_check=True)

            def passes(dst, wh, wl, xh, xl, start, stop):
                mm(dst, wh, xh, start, False)
                mm(dst, wh, xl, False, False)
                return mm(dst, wl, xh, False, stop)

            def unit(dst, u, xh, xl, nk=8, k0=0, start=True, stop=True, ready=None):
                b, e = u
                s = b % SLOTS
                after(pe, split_lo, b + 1 + 3 * e)
                for k in range(nk):
                    if ready:
                        ready(k0 + k)
                    last = passes(dst, w_hi[:, s, k, :], w_lo[:, s, k, :], xh[:, k0 + k, :], xl[:, k0 + k, :],
                                  start and k == 0, stop and k == nk - 1)
                last.then_inc(unit_used, 1)

            def together(units, ready):
                for _, u in units:
                    pe.wait_ge(split_lo, u + 1)
                for k in range(KT):
                    ready(k)
                    for dst, u in units:
                        last = passes(dst, w_hi[:, u % SLOTS, k, :], w_lo[:, u % SLOTS, k, :], h_hi[:, k, :],
                                      h_lo[:, k, :], k == 0, k == KT - 1)
                        if k == KT - 1:
                            last.then_inc(unit_used, 1)

            def modulation(ch, b):
                after(pe, acc_step, 8 * ch + 8)
                first = isinstance(ch, int) and ch < 4
                if not first:
                    after(pe, mod_w, ch)
                for j in range(4):
                    o = 4 * ch + j if first else j
                    last = mm(b[:, o:o + 1], (ACC[ch] if first else acc)[:, j * P:(j + 1) * P], ones[:, 0:1],
                              o == 0, True)
                last.then_inc(mod_sum, 1)

            def sum_squares(n):
                pe.wait_ge(sq_acc, (KT - 2) * n)
                mm(PA[:, :], ones[:, :], tmp[:, 0, :], True, False)
                pe.wait_ge(sq_w, KT * (n + 1))
                mm(PA[:, :], ones[:, :], sq[:, 1, :], False, True).then_inc(sq_sum, 1)

            def scores(l, p, s, h, hb, first=False):
                b = att[l]
                r = slice(DH * hb, DH * hb + DH)
                G = 8 * p + 4 * hb
                if hb == 0:
                    after(pe, qlo_w, NP * l + p + 1)
                    after(pe, klo_w, NP * l + p + 1)
                    if l == 1:
                        pe.wait_ge(frow_in[s], 32 * (h + 1))
                        if first:
                            pe.wait_ge(vlo_w, NP + 1)
                for i in range(HB):
                    if l == 0:
                        after(pe, phi_w, G + i - 3)
                        n = SPAN[i]
                        passes(Z[i][:, 0:n], b["k_hi"][r, s, i * P:(i + 1) * P], b["k_lo"][r, s, i * P:(i + 1) * P],
                               b["q_hi"][r, s, i * P:S], b["q_lo"][r, s, i * P:S], True, False)
                        mm(Z[i][:, 0:P], ident_r[:, :], maskS_r[:, :], False, True).then_inc(z_sum, 1)
                    else:
                        after(pe, plo_w, 8 * NP + G + i - 3)
                        n = P * (i + 1)
                        passes(Z[i][:, 0:n], b["q_hi"][r, s, i * P:(i + 1) * P], b["q_lo"][r, s, i * P:(i + 1) * P],
                               b["k_hi"][r, s, 0:n], b["k_lo"][r, s, 0:n], True, False)
                        mm(Z[i][:, 0:n], ones_r[32 * hb:32 * hb + 2, :], frow[32 * hb:32 * hb + 2, s, 0:n], False, False)
                        mm(Z[i][:, n - P:n], ident_r[:, :], maskF_r[:, :], False, True).then_inc(z_sum, 1)

            def middle(l, p, hb):
                G = 8 * p + 4 * hb
                if l == 0:
                    after(pe, softlo_w, G + HB)
                    for i in range(HB):
                        for j in range(i, HB):
                            w = negtri_r if i == j else negones_r
                            dst = Z[i][:, P * (j - i):SPAN[i]]
                            o = slice(OFF[j], OFF[j] + SPAN[j])
                            mm(dst, w[:, :], soft_hi[:, o], False, False)
                            last = mm(dst, w[:, :], soft_lo[:, o], False, j == HB - 1)
                        last.then_inc(r_sum, 1)
                else:
                    after(pe, p_norm, G + HB)
                    for j in range(HB):
                        for i in range(j, HB):
                            o = P * (i * (i + 1) // 2 + j)
                            last = nc.tensor.transpose(Z[j][:, P * (i - j):P * (i - j + 1)], prob[:, o:o + P],
                                                       ident[:, :])
                        last.then_inc(r_sum, 1)

            def weigh(l, p, s, hb):
                b = att[l]
                G = 8 * p + 4 * hb
                if hb == 0:
                    after(pe, vlo_w, NP * l + p + 1)
                    if l == 1:
                        pe.wait_ge(f_y, 1)
                after(pe, olo_w, 2 * NP * l + 2 * p + (1 if hb else -1))
                if l == 1 and hb == 1 and not (isinstance(p, int) and p == NP - 1):
                    after(pe, qk_ln, 2 * p + 4)
                for i in range(HB):
                    after(pe, plo_w, 8 * NP * l + G + i + 1)
                    o = slice(i * P, (i + 1) * P)
                    passes(OB[hb][:, i * P:S], b["v_hi"][:, s, o], b["v_lo"][:, s, o],
                           b["p_hi"][:, AT[i]], b["p_lo"][:, AT[i]], i == 0, i == HB - 1
                           ).then_inc(pv, 1)

            def project_q(l, p):
                after(pe, vT_w, NP * l + p)
                if l == 0:
                    after(pe, mod_w, p + 3)
                unit(PA[:, :], (U_L * l, p), h_hi, h_lo)

            def sum_q(l, p):
                if l == 1:
                    after(pe, qk_sq, 2 * p + 1)
                    after(pe, olo_w, 2 * NP + 2 * (p - 1))
                    mm(OB[1][:, :], headones[:, :], sq[:, 0, :], True, True).then_inc(qk_sum, 1)

            def project_k(l, p):
                after(pe, vlo_w, NP * l + p)
                unit(PB[:, :], (U_L * l + 1, p), hk_hi if l else h_hi, hk_lo if l else h_lo)

            def sum_k(l, p):
                if l == 1:
                    after(pe, qk_sq, 2 * p + 2)
                    after(pe, qk_ln, 2 * p + 1)
                    mm(OB[1][:, :], headones[:, :], sq[:, 0, :], True, True).then_inc(qk_sum, 1)

            def project_v(l, p):
                after(pe, qk_n if l else qlo_w, 2 * p + 1 if l else p + 1)
                unit(PA[:, :], (U_L * l + 2, p), hk_hi if l else h_hi, hk_lo if l else h_lo)

            def transpose_v(l, p, b=PB):
                after(pe, vT_w, NP * l + p + 1)
                if b is PB:
                    after(pe, qk_n if l else klo_w, 2 * p + 2 if l else p + 1)
                for i in range(TB):
                    last = nc.tensor.transpose(b[:, i * P:(i + 1) * P], sq[:, 1, i * P:(i + 1) * P], ident[:, :])
                last.then_inc(v_T, 1)

            def mix(l, t, k0, k1):
                u = U_L * l + U_O + t
                if k0 == 0:
                    pe.wait_ge(split_lo, u + 1)
                    if t == 0:
                        after(pe, vT_w, NP * (l + 1))
                        if l == 0:
                            pe.wait_ge(mod_w, NP + 3)
                    elif t == 1:
                        pe.wait_ge(vlo_w, NP * (l + 1))
                    elif t > 4:
                        pe.wait_ge(x_ready, KT * (2 * l + 1) + t - 2)
                b, s = MIX_BANK[t], u % SLOTS
                for k in range(k0, k1):
                    if t == 0:
                        pe.wait_ge(olo_w, 2 * NP * l + 2 * (k + 1))
                    last = passes(b[:, :], w_hi[:, s, k, :], w_lo[:, s, k, :], att[l]["o_hi"][:, k, :],
                                  att[l]["o_lo"][:, k, :], k == 0, k == KT - 1)
                if k1 == KT:
                    last.then_inc(unit_used, 1)

            def transpose_y(t):
                pe.wait_ge(x_ready, KT * 4 + t + 1)
                after(pe, y_w, t - 3)
                for b in range(TB):
                    last = nc.tensor.transpose(y_bank(t, b)[:, b * P:(b + 1) * P], xT[:, t, b * P:(b + 1) * P],
                                               ident[:, :])
                last.then_inc(y_T, 1)

            def step(l, p, s, h, first=False, last=False):
                scores(l, p, s, h, 0, first)
                if not first:
                    weigh(l, p - 1, 1 - s, 1)
                if last:
                    mix(l, 0, 0, NP - 2)
                else:
                    project_q(l, p + 1)
                middle(l, p, 0)
                if last:
                    mix(l, 1, 0, 3)
                else:
                    sum_q(l, p + 1)
                    project_k(l, p + 1)
                scores(l, p, s, h, 1)
                if not last:
                    sum_k(l, p + 1)
                weigh(l, p, s, 0)
                if last:
                    mix(l, 1, 3, NP - 2)
                    mix(l, 0, NP - 2, NP - 1)
                    mix(l, 1, NP - 2, NP - 1)
                else:
                    project_v(l, p + 1)
                middle(l, p, 1)
                if not last:
                    transpose_v(l, p + 1)
                    if l == 0:
                        modulation(p + 4, PA)

            pe.wait_ge(consts, 5)
            pe.wait_ge(rows_in, 16 * 12)
            nc.tensor.transpose(Z[0][:, 0:NM], rows1[0:NM, :], ident[0:NM, 0:NM]).then_inc(rows_T, 1)
            nc.tensor.transpose(Z[1][:, 0:NG], rows2[0:NG, :], ident[0:NG, 0:NG]).then_inc(rows_T, 1)
            pe.wait_ge(x_in, 16)
            for t in range(KT + 2):
                if t < KT:
                    after(pe, x_ready, t - 1)
                    for b in range(TB):
                        last = nc.tensor.transpose(OB[t % 2][:, b * P:(b + 1) * P],
                                                   x_nat[:, b, t * P:(t + 1) * P], ident[:, :])
                    last.then_inc(x_T, 1)
                if t >= 2:
                    pe.wait_ge(sq_w, t - 1)
                    mm(PA[:, :], ones[:, :], sq[:, t % 2, :], t == 2, t == KT + 1).then_inc(sq_sum, 1)
            pe.wait_ge(consts, N_CONSTS)
            for ch in range(4):
                modulation(ch, PB)

            for l in range(2):
                base = U_L * l
                hb0, hb1 = HBASE[2 * l], HBASE[2 * l + 1]

                if l == 0:
                    pe.wait_ge(mod_w, 4)
                    together([(PA[:, :], 0), (PB[:, :], 1)], lambda k: pe.wait_ge(hlo_w, k + 1))
                    project_v(0, 0)
                    transpose_v(0, 0)
                else:
                    pe.wait_ge(wfs_lo, 1)
                    pe.wait_ge(split_lo, base + 1)
                    pe.wait_ge(mod_w, ADA_N)
                    dst = ((OB[0], wf_hi, wf_lo), (PB, w_hi[:, base % SLOTS], w_lo[:, base % SLOTS]))
                    for k in range(KT):
                        pe.wait_ge(hlo_w, hb0 + k + 1)
                        for b, (bk, wh, wl) in enumerate(dst):
                            last = passes(bk[:, :], wh[:, k, :], wl[:, k, :], hk_hi[:, k, :], hk_lo[:, k, :],
                                          k == 0, k == KT - 1)
                            if k == KT - 1:
                                last.then_inc(unit_used if b else f_sum, 1)
                    unit(Z[2][:, :], (base + 1, 0), hk_hi, hk_lo)
                    pe.wait_ge(qk_sq, 1)
                    mm(Z[0][:, :], headones[:, :], sq[:, 0, :], True, True).then_inc(qk_sum, 1)
                    transpose_v(1, 0, Z[3])
                    unit(PA[:, :], (base + 2, 0), h_hi, h_lo, ready=lambda k: pe.wait_ge(hlo_w, hb0 + KT + k + 1))
                    pe.wait_ge(qk_sq, 2)
                    mm(Z[1][:, :], headones[:, :], sq[:, 0, :], True, True).then_inc(qk_sum, 1)
                step(l, 0, 0, 0, first=True)
                with pe.Fori(0, NP // 2 - 1) as i:
                    step(l, 2 * i + 1, 1, i)
                    step(l, 2 * i + 2, 0, i + 1)
                step(l, NP - 1, 1, NP // 2 - 1, last=True)
                weigh(l, NP - 1, 1, 1)

                mix(l, 0, NP - 1, NP)
                mix(l, 2, 0, NP - 1)
                mix(l, 1, NP - 1, NP)
                mix(l, 2, NP - 1, NP)
                for t in range(3, KT):
                    if l == 0 and t in (3, 5):
                        pe.wait_ge(x_ready, KT + 2)
                        modulation(NP + 3 + t // 2 - 1, PB)
                    mix(l, t, 0, KT)
                sum_squares(2 * l + 1)
                if l == 0:
                    modulation(NP + 5, PB)

                def feed(u, e, r, free, ch=None):
                    after(pe, m_w, free)
                    unit(bank[2 + 2 * r][:, :], (u, e), h_hi, h_lo)
                    if ch is not None:
                        modulation(ch, PB)
                    unit(bank[3 + 2 * r][:, :], (u + 1, e), h_hi, h_lo)

                def feed3(i):
                    for r in range(3):
                        feed(base + U_F + 2 + 2 * r, 2 * i, r, FT * l + 3 * i + max(r - 1, 0),
                             ch=i + ADA_F if l == 0 and r == 2 else None)
                together([(bank[6][:, :], base + U_F), (bank[7][:, :], base + U_F + 1)],
                         lambda k: pe.wait_ge(hlo_w, hb1 + k + 1))
                feed3(0)
                with pe.Fori(1, FT // 3) as i:
                    feed3(i)

                m_hi, m_lo = mid[l]

                def down(t, s, first=False):
                    if l == 1 and isinstance(t, int) and t == KT - 1:
                        for j in range(KT - 2):
                            transpose_y(j)
                    if not first:
                        pe.wait_ge(x_ready, KT * (2 * l + 2) + t - 1)
                    for j, (k0, k1) in enumerate(((0, 8), (8, 16), (16, FT))):
                        if l == 0 and j == 1 and not first and not (isinstance(t, int) and t == KT - 1):
                            modulation(t + ADA_D - 1, PB)
                        if l == 1 and j == 2 and isinstance(t, int) and t == KT - 1:
                            transpose_y(KT - 2)
                        unit(bank[2 + s][:, :], (base + U_D + j, t), m_hi, m_lo, k1 - k0, k0, j == 0, j == 2,
                             ready=(lambda k: pe.wait_ge(mlo_w, FT * l + k + 1)) if first else None)

                down(0, 0, True)
                with pe.Fori(0, KT // 2 - 1) as i:
                    down(2 * i + 1, 1)
                    down(2 * i + 2, 0)
                down(KT - 1, 1)
                if l == 0:
                    sum_squares(2)
                    modulation(ADA_N - 1, PB)

            transpose_y(KT - 1)

        @block.scalar
        def _(act):
            A = nc.scalar.activation

            def exp_ln_tables():
                act.add_instruction(mybir.InstLoadActFuncSet(name=nc.get_next_instruction_name(),
                                                             act_func_set_id=EXP_LN_SET, ins=[], outs=[]))

            def split(u):
                b, e = u
                s = b % SLOTS
                after(act, unit_used, b - 2 + 3 * e)
                after(act, raw_in[s], 16 * (b // SLOTS + 1 + e))
                nc.scalar.copy(w_hi[:, s, :, :], raw[:, s, :, :]).then_inc(split_hi, 1)

            def square(n, t, s):
                after(act, x_ready, KT * n + t + 1)
                if n == 0:
                    after(act, sq_sum, t - 1)
                elif not isinstance(t, int) or t > 2:
                    act.wait_ge(sq_acc, (KT - 2) * (n - 1) + t - 2)
                src = xT[:, t, :] if isinstance(t, int) else xT[:, DSL(t, 1), :].rearrange("q a s -> q (a s)")
                dst = tmp[:, 0, :] if n > 0 and isinstance(t, int) and t == 0 else sq[:, s, :]
                A(dst, src, ACT.Square).then_inc(sq_w, 1)

            def norm(n, between=None):
                act.wait_ge(sq_sum, KT + n)
                A(rstd[:, :], PA[:, :], ACT.Ln, bias=epsc[:, 0:1], scale=1.0 / D).then_inc(rs_ln, 1)
                act.wait_ge(rs_ln, n + 1)
                A(rstd[:, :], rstd[:, :], ACT.Exp, scale=-0.5).then_inc(rs_w, 1)
                sets = {0: [(M_SHA, h_hi)], 1: [(M_SHF, h_hi)], 2: [(M_KVSH, hk_hi), (M_L1 + M_SHA, h_hi)],
                        3: [(M_L1 + M_SHF, h_hi)]}[n]
                for m, (sh, hi) in enumerate(sets):
                    for t in range(KT):
                        act.wait_ge(ht_w, HBASE[n] + KT * m + t + 1)
                        A(hi[:, t, :], tmp[:, t % 2, :], ACT.Identity,
                          bias=mods[:, sh + t:sh + t + 1]).then_inc(hhi_w, 1)
                        if m == 1:
                            between(t)

            def chain(l, p, hb):
                G = 8 * p + 4 * hb
                if l == 0:
                    for i in range(HB):
                        after(act, z_sum, G + i + 1)
                        after(act, softlo_w, G + i - 3)
                        A(soft[:, AT[i]], Z[i][:, 0:SPAN[i]], ACT.Abs).then_inc(z_abs, 1)
                    for i in range(HB):
                        after(act, z_abs, G + i + 1)
                        A(soft[:, AT[i]], soft[:, AT[i]], ACT.Exp, scale=-1.0).then_inc(z_exp, 1)
                    for i in range(HB):
                        after(act, z_exp, G + i + 1)
                        A(soft[:, AT[i]], soft[:, AT[i]], ACT.Ln, bias=1.0).then_inc(z_ln, 1)
                else:
                    after(act, negmax_w, 2 * p + hb + 1)
                    after(act, r_sum, 8 * NP + G)
                    for i in range(HB):
                        o = P * (i * (i + 1) // 2)
                        A(prob[:, o:o + P * (i + 1)], Z[i][:, 0:P * (i + 1)], ACT.Exp, bias=stat[:, 1, i:i + 1],
                          accum_out=stat[:, 2, i:i + 1]).then_inc(p_exp, 1)

            def soft_highs(l, p, hb):
                G = 8 * p + 4 * hb
                for i in range(HB if l == 0 else 0):
                    after(act, soft_w, G + i + 1)
                    after(act, r_sum, G + i - 3)
                    nc.scalar.copy(soft_hi[:, AT[i]], soft[:, AT[i]]).then_inc(softhi_w, 1)

            def weights(l, p, hb):
                G = 8 * p + 4 * hb
                for i in range(HB):
                    after(act, r_sum, 8 * NP * l + G + i + 1)
                    after(act, pv, 8 * NP * l + G + i - 3)
                    if l == 0:
                        A(wgt[:, AT[i]], Z[i][:, 0:SPAN[i]], ACT.Exp)
                        A(att[0]["p_hi"][:, AT[i]], Z[i][:, 0:SPAN[i]], ACT.Exp).then_inc(phi_w, 1)
                    else:
                        nc.scalar.copy(att[1]["p_hi"][:, AT[i]], Z[i][:, 0:SPAN[i]]).then_inc(phi_w, 1)

            def out_hi(l, p, hb):
                r = slice(DH * hb, DH * hb + DH)
                after(act, pv, 8 * NP * l + 8 * p + 4 * hb + HB)
                dst = att[l]["o_hi"]
                dst = dst[r, p, :] if isinstance(p, int) else dst[r, DSL(p, 1), :].rearrange("q a s -> q (a s)")
                nc.scalar.copy(dst, OB[hb][r, :]).then_inc(ohi_w, 1)

            def q_first(l, p, s):
                after(act, unit_used, U_L * l + 3 * p + 1)
                if l == 0:
                    A(att[0]["q_hi"][:, s, :], PA[:, :], ACT.Copy, scale=DH ** -0.5).then_inc(qhi_w, 1)
                else:
                    A(sq[:, 0, :], PA[:, :], ACT.Square).then_inc(qk_sq, 1)

            def k_first(l, p, s):
                after(act, unit_used, U_L * l + 3 * p + 2)
                if l == 0:
                    nc.scalar.copy(att[0]["k_hi"][:, s, :], PB[:, :]).then_inc(khi_w, 1)
                else:
                    A(sq[:, 0, :], PB[:, :], ACT.Square).then_inc(qk_sq, 1)

            def head_ln(l, p, j):
                if l == 0:
                    return
                after(act, qk_sum, 2 * p + j + 1)
                A(rstd[:, :], OB[1][:, :], ACT.Ln, bias=epsc[:, 0:1], scale=1.0 / DH).then_inc(qk_ln, 1)

            def head_norm(l, p, s, j):
                if l == 0:
                    return
                n = 2 * p + j + 1
                after(act, qk_ln, n)
                A(rstd[:, :], rstd[:, :], ACT.Exp, scale=-0.5).then_inc(qk_rs, 1)
                after(act, qk_n, n)
                nc.scalar.copy(att[1]["k_hi" if j else "q_hi"][:, s, :], tmp[:, j, :]).then_inc(khi_w if j else qhi_w, 1)

            def v_rows(l, p):
                after(act, unit_used, U_L * l + 3 * p + 3)
                nc.scalar.copy(sq[:, 1, :], PA[:, :]).then_inc(vT_w, 1)

            def v_last(l, p, s):
                after(act, v_T, NP * l + p + 1)
                nc.scalar.copy(att[l]["v_hi"][:, s, :], PB[:, :]).then_inc(vhi_w, 1)

            def step(l, p, s, first=False, last=False):
                base = U_L * l
                chain(l, p, 0)
                if not first:
                    out_hi(l, p - 1, 1)
                soft_highs(l, p, 0)
                if not last:
                    q_first(l, p + 1, 1 - s)
                    if l == 0:
                        split((base, p + 2))
                weights(l, p, 0)
                if not last:
                    head_ln(l, p + 1, 0)
                    head_norm(l, p + 1, 1 - s, 0)
                    if l == 1:
                        split((base, p + 2))
                    k_first(l, p + 1, 1 - s)
                    head_ln(l, p + 1, 1)
                    if l == 0:
                        split((base + 1, p + 2))
                chain(l, p, 1)
                if not last:
                    head_norm(l, p + 1, 1 - s, 1)
                out_hi(l, p, 0)
                soft_highs(l, p, 1)
                if not last:
                    if l == 1:
                        split((base + 1, p + 2))
                    v_rows(l, p + 1)
                weights(l, p, 1)
                if not last:
                    v_last(l, p + 1, 1 - s)
                    split((base + 2, p + 2))

            exp_ln_tables()
            load_rows(act, 0)
            act.wait_ge(cols_w, 2)
            A(cact[:, 0, :], gains[:, G_C:G_C + KT], ACT.Exp, scale=-1.0).then_inc(silu_c, 1)
            for t in range(KT + 1):
                if t < KT:
                    act.wait_ge(x_T, t + 1)
                    nc.scalar.copy(xT[:, t, :], OB[t % 2][:, :]).then_inc(x_ready, 1)
                if t > 0:
                    square(0, t - 1, (t - 1) % 2)
            for j in range(3):
                split((j, 0))

            for l in range(2):
                base = U_L * l
                if l == 0:
                    norm(0)
                    q_first(0, 0, 0)
                    k_first(0, 0, 0)
                    split((0, 1))
                    split((1, 1))
                    v_rows(0, 0)
                    split((2, 1))
                    v_last(0, 0, 0)
                else:
                    def between(t):
                        if t == 1:
                            act.wait_ge(f_y, 1)
                            A(f_soft, f_relu, ACT.Abs).then_inc(f_act, 1)
                        if t == 2:
                            act.wait_ge(unit_used, base + 1)
                            A(sq[:, 0, :], PB[:, :], ACT.Square).then_inc(qk_sq, 1)
                            act.wait_ge(f_act, 1)
                            A(f_soft, f_soft, ACT.Exp, scale=-1.0).then_inc(f_act, 1)
                        if t == 3:
                            act.wait_ge(f_act, 2)
                            A(f_soft, f_soft, ACT.Ln, bias=1.0).then_inc(f_act, 1)
                        if t == 4:
                            act.wait_ge(unit_used, base + 2)
                            nc.scalar.copy(sq[:, 1, :], Z[2][:, :]).then_inc(vT_w, 1)
                        if t == 5:
                            act.wait_ge(f_dve, 2)
                            nc.scalar.copy(f_hi, f_relu).then_inc(f_act, 1)
                        if t == 6:
                            act.wait_ge(qk_sum, 1)
                            act.wait_ge(f_split, 1)
                            A(k_rstd, Z[0][:, :], ACT.Ln, bias=epsc[:, 0:1], scale=1.0 / DH).then_inc(qk_ln, 1)
                        if t == 7:
                            act.wait_ge(qk_ln, 1)
                            A(k_rstd, k_rstd, ACT.Exp, scale=-0.5).then_inc(qk_rs, 1)
                    norm(2, between)
                    act.wait_ge(qk_n, 1)
                    nc.scalar.copy(att[1]["k_hi"][:, 0, :], tmp[:, 1, :]).then_inc(khi_w, 1)
                    act.wait_ge(unit_used, base + 3)
                    act.wait_ge(qk_sum, 1)
                    A(sq[:, 0, :], PA[:, :], ACT.Square).then_inc(qk_sq, 1)
                    act.wait_ge(v_T, NP + 1)
                    nc.scalar.copy(att[1]["v_hi"][:, 0, :], Z[3][:, :]).then_inc(vhi_w, 1)
                    act.wait_ge(qk_sum, 2)
                    A(rstd[:, :], Z[1][:, :], ACT.Ln, bias=epsc[:, 0:1], scale=1.0 / DH).then_inc(qk_ln, 1)
                    act.wait_ge(qk_ln, 2)
                    A(rstd[:, :], rstd[:, :], ACT.Exp, scale=-0.5).then_inc(qk_rs, 1)
                    split((base, 1))
                    act.wait_ge(qk_n, 2)
                    nc.scalar.copy(att[1]["q_hi"][:, 0, :], tmp[:, 0, :]).then_inc(qhi_w, 1)
                    split((base + 1, 1))
                    split((base + 2, 1))
                step(l, 0, 0, first=True)
                with act.Fori(0, NP // 2 - 1) as i:
                    step(l, 2 * i + 1, 1)
                    step(l, 2 * i + 2, 0)
                step(l, NP - 1, 1, last=True)
                out_hi(l, NP - 1, 1)

                for t in range(KT):
                    split((base + U_O + 3 + t, 0))
                    square(2 * l + 1, t, t % 2)
                norm(2 * l + 1)

                def feed(u, e, n, r):
                    b = (tmp[:, 0, :], tmp[:, 1, :], sq[:, 0, :])[r]
                    after(act, unit_used, u + 1 + 3 * e)
                    after(act, mlo_w, n - 2)
                    A(b, bank[2 + 2 * r][:, :], ACT.Silu).then_inc(silu_w, 1)
                    split((u + 3, e))
                    after(act, m_w, n + 1)
                    f = n - FT * l
                    dst = mid[l][0]
                    dst = dst[:, f, :] if isinstance(f, int) else dst[:, DSL(f, 1), :].rearrange("q a s -> q (a s)")
                    nc.scalar.copy(dst, b).then_inc(mhi_w, 1)
                    split((u + 4, e))

                def feed3(i):
                    for r in range(3):
                        feed(base + U_F + 2 + 2 * r, 2 * i, FT * l + 3 * i + 1 + r, r)
                feed(base + U_F, 0, FT * l, 2)
                feed3(0)
                with act.Fori(1, FT // 3) as i:
                    feed3(i)

                def down(t, s, more=3):
                    for j in range(more):
                        split((base + U_D + 3 + j, t))
                    if l == 0 and isinstance(t, int) and t == KT - 1:
                        act.wait_ge(wf_in, 16)
                        act.wait_ge(wf_zero, 2)
                        nc.scalar.copy(wf_hi[:, :, 0:H], wf_raw[:, :, :]).then_inc(wfs_hi, 1)
                        exp_ln_tables()
                    if l == 0:
                        square(2, t, s)
                down(0, 0)
                with act.Fori(0, KT // 2 - 1) as i:
                    down(2 * i + 1, 1)
                    down(2 * i + 2, 0)
                down(KT - 1, 1, more=3 if l == 0 else 0)
            for t in range(KT):
                act.wait_ge(y_T, t + 1)
                y_out(nc.scalar.copy, t, 0, TB if t < KT - 1 else 2).then_inc(y_w, 1)

        @block.vector
        def _(dve):
            V = nc.vector

            def split(u):
                b, e = u
                s = b % SLOTS
                after(dve, split_hi, b + 1 + 3 * e)
                V.tensor_tensor(w_lo[:, s, :, :], raw[:, s, :, :], w_hi[:, s, :, :].bitcast(F32),
                                ALU.subtract).then_inc(split_lo, 1)

            def lo(dst, v, hi):
                return V.tensor_tensor(dst, v, hi.bitcast(F32), ALU.subtract)

            def ada_chunk(ch, parts=range(4)):
                for o in range(2 * parts[0], 2 * parts[-1] + 2):
                    r, k = o // 2, o % 2
                    if k == 0:
                        after(dve, ada_in[r], 16 * (ch - 3))
                    cc = cact[:, 1, o:o + 1]
                    if o == 0:
                        after(dve, mod_sum, ch)
                        V.tensor_scalar(acc[:, :], ada[:, r, k, :], cc, None, ALU.mult).then_inc(acc_step, 1)
                    else:
                        after(dve, acc_step, 8 * ch + o)
                        V.scalar_tensor_tensor(acc[:, :], ada[:, r, k, :], cc, acc[:, :], ALU.mult,
                                               ALU.add).then_inc(acc_step, 1)

            def mods_out(ch, b):
                after(dve, mod_sum, ch + 1)
                o = slice(4 * ch, 4 * ch + 4) if isinstance(ch, int) else DSL(4 * ch, 4)
                V.tensor_tensor(mods[:, o], b[:, 0:4], mod_bias[:, o], ALU.add).then_inc(mod_w, 1)

            def gain(j, sc, g):
                V.scalar_tensor_tensor(amod[:, j, :], mods[:, sc:sc + KT], 1.0, gains[:, g:g + KT], ALU.add,
                                       ALU.mult).then_inc(amod_w, 1)

            def norm(n, between=None):
                sets = {0: [(0, M_SHA, h_hi, h_lo)], 1: [(1, M_SHF, h_hi, h_lo)],
                        2: [(3, M_KVSH, hk_hi, hk_lo), (2, M_L1 + M_SHA, h_hi, h_lo)],
                        3: [(4, M_L1 + M_SHF, h_hi, h_lo)]}[n]
                dve.wait_ge(rs_w, n + 1)

                def modulated(m, t):
                    if KT * m + t >= 2:
                        dve.wait_ge(hlo_w, HBASE[n] + KT * m + t - 1)
                    V.scalar_tensor_tensor(tmp[:, t % 2, :], xT[:, t, :], amod[:, sets[m][0], t:t + 1], rstd[:, :],
                                           ALU.mult, ALU.mult).then_inc(ht_w, 1)

                def low(m, t):
                    _, sh, hi, lo_ = sets[m]
                    dve.wait_ge(hhi_w, HBASE[n] + KT * m + t + 1)
                    V.scalar_tensor_tensor(lo_[:, t, :], tmp[:, t % 2, :], mods[:, sh + t:sh + t + 1],
                                           hi[:, t, :].bitcast(F32), ALU.add, ALU.subtract).then_inc(hlo_w, 1)
                order = [(m, t) for m in range(len(sets)) for t in range(KT)]
                modulated(*order[0])
                for a, b in zip(order, order[1:] + [None]):
                    if b:
                        modulated(*b)
                    low(*a)
                    if a[0] == 1:
                        between(a[1])

            def add_squares(n, t, s):
                after(dve, sq_w, KT * n + t + 1)
                if not isinstance(t, int) or t > 1:
                    dve.wait_ge(sq_acc, (KT - 2) * (n - 1) + t - 1)
                V.tensor_tensor(tmp[:, 0, :], tmp[:, 0, :], sq[:, s, :], ALU.add).then_inc(sq_acc, 1)

            def add_x(stage, t, src, unit_n, g):
                after(dve, unit_used, unit_n)
                if isinstance(t, int):
                    d, gc = xT[:, t, :], mods[:, g + t:g + t + 1]
                else:
                    d, gc = xT[:, DSL(t, 1), :].rearrange("q a s -> q (a s)"), mods[:, DSL(t + g, 1)]
                V.scalar_tensor_tensor(d, src, gc, d, ALU.mult, ALU.add).then_inc(x_ready, 1)

            def chain(l, p, hb):
                G = 8 * p + 4 * hb
                if l == 0:
                    for i in range(HB):
                        after(dve, z_ln, G + i + 1)
                        V.scalar_tensor_tensor(soft[:, AT[i]], Z[i][:, 0:SPAN[i]], 0.0, soft[:, AT[i]], ALU.max,
                                               ALU.add).then_inc(soft_w, 1)
                    for i in range(HB):
                        after(dve, softhi_w, G + i + 1)
                        lo(soft_lo[:, AT[i]], soft[:, AT[i]], soft_hi[:, AT[i]]).then_inc(softlo_w, 1)
                else:
                    for i in range(HB):
                        after(dve, z_sum, 8 * NP + G + i + 1)
                        V.reduce_max(stat[:, 0, i:i + 1], Z[i][:, 0:P * (i + 1)], AX.X).then_inc(max_w, 1)
                    after(dve, max_w, G + HB)
                    V.tensor_scalar(stat[:, 1, :], stat[:, 0, :], -1.0, None, ALU.mult).then_inc(negmax_w, 1)
                    after(dve, p_exp, G + HB)
                    V.reciprocal(stat[:, 3, :], stat[:, 2, :]).then_inc(inv_w, 1)
                    after(dve, inv_w, 2 * p + hb + 1)
                    for i in range(HB):
                        o = P * (i * (i + 1) // 2)
                        V.tensor_scalar(prob[:, o:o + P * (i + 1)], prob[:, o:o + P * (i + 1)], stat[:, 3, i:i + 1],
                                        None, ALU.mult).then_inc(p_norm, 1)

            def weights(l, p, hb):
                G = 8 * p + 4 * hb
                b = att[l]
                for i in range(HB):
                    after(dve, phi_w, 8 * NP * l + G + i + 1)
                    src = Z[i][:, 0:SPAN[i]] if l else wgt[:, AT[i]]
                    lo(b["p_lo"][:, AT[i]], src, b["p_hi"][:, AT[i]]).then_inc(plo_w, 1)

            def out_lo(l, p, hb):
                r = slice(DH * hb, DH * hb + DH)
                after(dve, ohi_w, 2 * NP * l + 2 * p + hb + 1)
                hi, lo_ = att[l]["o_hi"], att[l]["o_lo"]
                if isinstance(p, int):
                    hi, lo_ = hi[r, p, :], lo_[r, p, :]
                else:
                    hi, lo_ = (t[r, DSL(p, 1), :].rearrange("q a s -> q (a s)") for t in (hi, lo_))
                lo(lo_, OB[hb][r, :], hi).then_inc(olo_w, 1)

            def q_last(l, p, s):
                b = att[l]
                if l == 0:
                    after(dve, qhi_w, p + 1)
                    V.scalar_tensor_tensor(b["q_lo"][:, s, :], PA[:, :], DH ** -0.5, b["q_hi"][:, s, :].bitcast(F32),
                                           ALU.mult, ALU.subtract).then_inc(qlo_w, 1)
                else:
                    after(dve, qk_rs, 2 * p + 1)
                    V.scalar_tensor_tensor(tmp[:, 0, :], PA[:, :], gains[:, G_Q:G_Q + 1], rstd[:, :], ALU.mult,
                                           ALU.mult).then_inc(qk_n, 1)
                    after(dve, qhi_w, NP + p + 1)
                    lo(b["q_lo"][:, s, :], tmp[:, 0, :], b["q_hi"][:, s, :]).then_inc(qlo_w, 1)

            def k_last(l, p, s):
                b = att[l]
                if l == 0:
                    after(dve, khi_w, p + 1)
                    lo(b["k_lo"][:, s, :], PB[:, :], b["k_hi"][:, s, :]).then_inc(klo_w, 1)
                else:
                    after(dve, qk_rs, 2 * p + 2)
                    V.scalar_tensor_tensor(tmp[:, 1, :], PB[:, :], gains[:, G_K:G_K + 1], rstd[:, :], ALU.mult,
                                           ALU.mult).then_inc(qk_n, 1)
                    after(dve, khi_w, NP + p + 1)
                    lo(b["k_lo"][:, s, :], tmp[:, 1, :], b["k_hi"][:, s, :]).then_inc(klo_w, 1)

            def v_last(l, p, s):
                after(dve, vhi_w, NP * l + p + 1)
                lo(att[l]["v_lo"][:, s, :], PB[:, :], att[l]["v_hi"][:, s, :]).then_inc(vlo_w, 1)

            def step(l, p, s, first=False, last=False):
                base = U_L * l

                def ada_part(r):
                    if l == 0:
                        ada_chunk(p + 4, [r])
                ada_part(0)
                chain(l, p, 0)
                if not first:
                    out_lo(l, p - 1, 1)
                if not last and l == 0:
                    q_last(l, p + 1, 1 - s)
                    split((base, p + 2))
                ada_part(1)
                weights(l, p, 0)
                if not last and l == 0:
                    k_last(l, p + 1, 1 - s)
                    split((base + 1, p + 2))
                if not last and l == 1:
                    q_last(l, p + 1, 1 - s)
                    split((base, p + 2))
                ada_part(2)
                chain(l, p, 1)
                if not last and l == 1:
                    k_last(l, p + 1, 1 - s)
                out_lo(l, p, 0)
                if not last and l == 1:
                    split((base + 1, p + 2))
                ada_part(3)
                weights(l, p, 1)
                if not last:
                    v_last(l, p + 1, 1 - s)
                    split((base + 2, p + 2))
                    if l == 0:
                        mods_out(p + 4, PA)

            dve.wait_ge(rows_T, 2)
            V.tensor_copy(mod_bias[:, :], Z[0][:, 0:NM]).then_inc(cols_w, 1)
            V.tensor_copy(gains[:, :], Z[1][:, 0:NG]).then_inc(cols_w, 1)
            dve.wait_ge(silu_c, 1)
            dve.wait_ge(cols_w, 2)
            V.tensor_scalar(cact[:, 0, :], cact[:, 0, :], 1.0, None, ALU.add).then_inc(silu_c, 1)
            dve.wait_ge(silu_c, 2)
            V.reciprocal(cact[:, 0, :], cact[:, 0, :]).then_inc(silu_c, 1)
            dve.wait_ge(silu_c, 3)
            V.tensor_tensor(cact[:, 1, :], cact[:, 0, :], gains[:, G_C:G_C + KT], ALU.mult).then_inc(silu_c, 1)
            V.tensor_scalar(gains[:, G_Q:G_Q + 1], gains[:, G_Q:G_Q + 1], DH ** -0.5, None, ALU.mult).then_inc(silu_c, 1)
            dve.wait_ge(silu_c, 5)
            for ch in range(4):
                for o in range(KT):
                    cc, src = cact[:, 1, o:o + 1], ada_first[:, ch, o, :]
                    if o % (KT // 2) == 0:
                        dve.wait_ge(first_in[ch][o // (KT // 2)], 16)
                    if o == 0:
                        if ch == 3:
                            dve.wait_ge(mod_sum, 1)
                        V.tensor_scalar(ACC[ch], src, cc, None, ALU.mult).then_inc(acc_step, 1)
                    else:
                        dve.wait_ge(acc_step, 8 * ch + o)
                        V.scalar_tensor_tensor(ACC[ch], src, cc, ACC[ch], ALU.mult, ALU.add).then_inc(acc_step, 1)
                    if ch > 1 and o == KT // 2 - 1:
                        split((ch - 2, 0))
            dve.wait_ge(mod_sum, 4)
            V.tensor_tensor(mods[:, 0:16], PB[:, 0:16], mod_bias[:, 0:16], ALU.add).then_inc(mod_w, 4)
            dve.wait_ge(mod_w, 4)
            gain(0, M_SCA, G_ATT)
            dve.wait_ge(amod_w, 1)

            for l in range(2):
                base = U_L * l
                if l == 0:
                    norm(0)
                    split((2, 0))
                    q_last(0, 0, 0)
                    k_last(0, 0, 0)
                    split((0, 1))
                    split((1, 1))
                    split((2, 1))
                    v_last(0, 0, 0)
                else:
                    mods_out(ADA_N - 1, PB)

                    def between(t):
                        if t == 0:
                            dve.wait_ge(f_sum, 1)
                            V.tensor_scalar(f_relu, OB[0][0:H, :], gains[0:H, G_BF:G_BF + 1], None,
                                            ALU.add).then_inc(f_y, 1)
                        if t == 1:
                            dve.wait_ge(f_act, 1)
                            V.tensor_scalar(f_relu, f_relu, -1.0, 0.0, ALU.mult, ALU.max).then_inc(f_dve, 1)
                        if t == 3:
                            dve.wait_ge(f_act, 3)
                            dve.wait_ge(f_dve, 1)
                            V.tensor_tensor_scan(f_relu, f_relu, f_soft, 0.0, ALU.add, ALU.add).then_inc(f_dve, 1)
                        if t == 5:
                            dve.wait_ge(f_act, 4)
                            lo(f_lo, f_relu, f_hi).then_inc(f_split, 1)
                        if t == 7:
                            dve.wait_ge(qk_rs, 1)
                            dve.wait_ge(hlo_w, HBASE[3])
                            V.scalar_tensor_tensor(tmp[:, 1, :], PB[:, :], gains[:, G_K:G_K + 1], k_rstd, ALU.mult,
                                                   ALU.mult).then_inc(qk_n, 1)
                    norm(2, between)
                    dve.wait_ge(khi_w, NP + 1)
                    lo(att[1]["k_lo"][:, 0, :], tmp[:, 1, :], att[1]["k_hi"][:, 0, :]).then_inc(klo_w, 1)
                    dve.wait_ge(vhi_w, NP + 1)
                    lo(att[1]["v_lo"][:, 0, :], Z[3][:, :], att[1]["v_hi"][:, 0, :]).then_inc(vlo_w, 1)
                    dve.wait_ge(qk_rs, 2)
                    V.scalar_tensor_tensor(tmp[:, 0, :], PA[:, :], gains[:, G_Q:G_Q + 1], rstd[:, :], ALU.mult,
                                           ALU.mult).then_inc(qk_n, 1)
                    dve.wait_ge(qhi_w, NP + 1)
                    lo(att[1]["q_lo"][:, 0, :], tmp[:, 0, :], att[1]["q_hi"][:, 0, :]).then_inc(qlo_w, 1)
                    for j in range(3):
                        split((base + j, 1))
                step(l, 0, 0, first=True)
                with dve.Fori(0, NP // 2 - 1) as i:
                    step(l, 2 * i + 1, 1)
                    step(l, 2 * i + 2, 0)
                step(l, NP - 1, 1, last=True)
                out_lo(l, NP - 1, 1)

                ml = M_L1 * l
                for t in range(KT):
                    add_x(2 * l + 1, t, MIX_BANK[t][:, :], base + U_O + t + 1, ml + M_GA)
                    split((base + U_O + 3 + t, 0))
                    if 0 < t < KT - 1:
                        add_squares(2 * l + 1, t, t % 2)
                    if l == 0 and t in (2, 4):
                        mods_out(NP + 2 + t // 2, PB)
                        ada_chunk(NP + 3 + t // 2)
                if l == 0:
                    gain(1, M_SCF, G_FFN)
                    dve.wait_ge(amod_w, 2)
                if l == 0:
                    mods_out(NP + 5, PB)
                norm(2 * l + 1)

                def feed(u, e, n, r, ch=None):
                    b = (tmp[:, 0, :], tmp[:, 1, :], sq[:, 0, :])[r]
                    split((u + 3, e))
                    after(dve, silu_w, n + 1)
                    after(dve, unit_used, u + 2 + 3 * e)
                    V.tensor_tensor(b, b, bank[3 + 2 * r][:, :], ALU.mult).then_inc(m_w, 1)
                    split_after = (u + 4, e)
                    f = n - FT * l
                    after(dve, mhi_w, n + 1)
                    hi, lo_ = mid[l]
                    if isinstance(f, int):
                        hi, lo_ = hi[:, f, :], lo_[:, f, :]
                    else:
                        hi, lo_ = (t[:, DSL(f, 1), :].rearrange("q a s -> q (a s)") for t in (hi, lo_))
                    lo(lo_, b, hi).then_inc(mlo_w, 1)
                    split(split_after)
                    if ch is not None and r == 0:
                        ada_chunk(ch)
                    if ch is not None and r == 2:
                        mods_out(ch, PB)

                def feed3(i):
                    for r in range(3):
                        feed(base + U_F + 2 + 2 * r, 2 * i, FT * l + 3 * i + 1 + r, r,
                             i + ADA_F if l == 0 else None)
                feed(base + U_F, 0, FT * l, 2)
                feed3(0)
                with dve.Fori(1, FT // 3) as i:
                    feed3(i)

                def down(t, s, more=3, take=True, make=True, add=True):
                    for j in range(min(more, 2)):
                        split((base + U_D + 3 + j, t))
                    if l == 0 and take:
                        mods_out(t + ADA_D - 1, PB)
                    if l == 0 and make:
                        ada_chunk(t + ADA_D)
                    add_x(2 * l + 2, t, bank[2 + s][:, :], base + U_D + 3 + 3 * t, ml + M_GF)
                    if more == 3:
                        split((base + U_D + 5, t))
                    if l == 0 and add:
                        add_squares(2, t, s)
                down(0, 0, take=False, add=False)
                with dve.Fori(0, KT // 2 - 1) as i:
                    down(2 * i + 1, 1)
                    down(2 * i + 2, 0)
                down(KT - 1, 1, more=3 if l == 0 else 0, take=False, make=False, add=False)
                if l == 0:
                    dve.wait_ge(wfs_hi, 1)
                    lo(wf_lo[:, :, 0:H], wf_raw[:, :, :], wf_hi[:, :, 0:H]).then_inc(wfs_lo, 1)
                    dve.wait_ge(mod_w, ADA_N - 1)
                    gain(2, M_L1 + M_SCA, G_ATT + KT)
                    gain(3, M_KVSC, G_KV)
                    gain(4, M_L1 + M_SCF, G_FFN + KT)
                    dve.wait_ge(amod_w, 5)

            dve.wait_ge(y_T, KT)
            y_out(V.tensor_copy, KT - 1, 2, TB).then_inc(y_last, 1)


_NAMES = ["x", "c", "ada_w", "ada_b", "norm_attn_g", "norm_ffn_g", "w_ffn_in", "w_ffn_down", "sb_w_qkv", "sb_w_o",
          "kv_ada_w", "kv_ada_b", "kv_norm_g", "w_kvf", "b_f", "k_norm_g", "fox_w_q", "q_norm_g", "fox_w_o"]


def kernel(**inputs):
    import numpy as np
    import concourse.bacc as bacc
    from concourse.bass_utils import run_bass_kernel_spmd

    nc = bacc.Bacc("TRN2", target_bir_lowering=False, num_devices=1)
    arrays = {n: np.ascontiguousarray(inputs[n]) for n in _NAMES}
    aps = [nc.dram_tensor(n, arrays[n].shape, F32, kind="ExternalInput").ap() for n in _NAMES]
    res = nc.dram_tensor("result", arrays["x"].shape, F32, kind="ExternalOutput").ap()
    build(nc, *aps, res)
    return run_bass_kernel_spmd(nc, [arrays], core_ids=[0]).results[0]["result"]
```
